# Optimizing a Trainium2 kernel written in Bass

```python
import jax, jax.numpy as jnp
from jax import lax
import numpy as np

D_MODEL = 1024
BATCH = 1
SEQ = 2048
DEPTH = 1
DEC_BATCH = 1
DEC_SEQ = 64
PAST_LEN = 512

CHUNK = 64
EPS = 1e-6
NEG_INF = -1e30

A_HEADS = 8
A_KV_HEADS = 2
A_HEAD_DIM = 64
A_GROUP = A_HEADS // A_KV_HEADS
A_WIDTH = A_HEADS * A_HEAD_DIM
A_KV_WIDTH = A_KV_HEADS * A_HEAD_DIM
WINDOW = 128
WIN_CHUNKS = WINDOW // CHUNK
ROPE_DIM = A_HEAD_DIM // 4
ROPE_THETA = 500000.0
ATTN_SCALE = A_HEAD_DIM ** -0.5

B_HEADS = 4
B_KEY_DIM = 128
B_VAL_DIM = 128
B_KEY_WIDTH = B_HEADS * B_KEY_DIM
B_WIDTH = B_HEADS * B_VAL_DIM

COL_SIZES = (A_WIDTH, A_KV_WIDTH, A_KV_WIDTH, A_WIDTH,
             B_KEY_WIDTH, B_KEY_WIDTH, B_WIDTH, B_WIDTH,
             D_MODEL, D_MODEL)
W_IN_COLS = (A_WIDTH + 2 * A_KV_WIDTH + A_WIDTH + 2 * B_KEY_WIDTH
             + 2 * B_WIDTH + 2 * D_MODEL)

kernel_name = 'hybrid_swa_sink_hgrn2_gated_merge_stream_step'

def rms_norm(x, g):
    xf = x.astype(jnp.float32)
    y = xf * lax.rsqrt(jnp.mean(xf * xf, axis=-1, keepdims=True) + EPS)
    return (y * g.astype(jnp.float32)).astype(x.dtype)

def apply_partial_rope(x, pos):
    half = ROPE_DIM // 2
    inv = jnp.power(ROPE_THETA, -jnp.arange(half, dtype=jnp.float32) * (2.0 / ROPE_DIM))
    ang = pos.astype(jnp.float32)[:, None] * inv[None, :]
    cos = jnp.cos(ang)[:, None, :]
    sin = jnp.sin(ang)[:, None, :]
    xr = x[..., :ROPE_DIM].astype(jnp.float32)
    x1, x2 = xr[..., :half], xr[..., half:]
    rot = jnp.concatenate([x1 * cos - x2 * sin, x2 * cos + x1 * sin], axis=-1)
    return jnp.concatenate([rot.astype(x.dtype), x[..., ROPE_DIM:]], axis=-1)

def split_projection(p):
    cuts = []
    acc = 0
    for s in COL_SIZES[:-1]:
        acc += s
        cuts.append(acc)
    return jnp.split(p, cuts, axis=-1)

def sink_softmax_attention(q, k, v, mask, sinks):
    s = jnp.einsum('...qhgd,...khd->...hgqk', q, k, preferred_element_type=jnp.float32) * ATTN_SCALE
    s = jnp.where(mask, s, NEG_INF)
    sink = jnp.broadcast_to(sinks.astype(jnp.float32).reshape(A_KV_HEADS, A_GROUP, 1, 1),
                            s.shape[:-1] + (1,))
    p = jax.nn.softmax(jnp.concatenate([s, sink], axis=-1), axis=-1)[..., :-1]
    return jnp.einsum('...hgqk,...khd->...qhgd', p.astype(v.dtype), v)

def window_attention_prompt(q, k, v, sinks):
    b, s = q.shape[:2]
    nc = s // CHUNK
    qc = q.reshape(b, nc, CHUNK, A_KV_HEADS, A_GROUP, A_HEAD_DIM)
    pad = ((0, 0), (WIN_CHUNKS - 1, 0), (0, 0), (0, 0), (0, 0))
    kp = jnp.pad(k.reshape(b, nc, CHUNK, A_KV_HEADS, A_HEAD_DIM), pad)
    vp = jnp.pad(v.reshape(b, nc, CHUNK, A_KV_HEADS, A_HEAD_DIM), pad)
    kb = jnp.concatenate([kp[:, j:j + nc] for j in range(WIN_CHUNKS)], axis=2)
    vb = jnp.concatenate([vp[:, j:j + nc] for j in range(WIN_CHUNKS)], axis=2)
    key_chunk = (jnp.arange(nc)[:, None] - (WIN_CHUNKS - 1)
                 + jnp.arange(WIN_CHUNKS * CHUNK)[None, :] // CHUNK)
    mask = (key_chunk >= 0)[:, None, None, None, :]
    o = sink_softmax_attention(qc, kb, vb, mask, sinks)
    return o.reshape(b, s, A_WIDTH)

def window_attention_sample(q, k, v, cache_k, cache_v, sinks):
    b, t = q.shape[:2]
    kb = jnp.concatenate([cache_k.astype(k.dtype), k], axis=1)
    vb = jnp.concatenate([cache_v.astype(v.dtype), v], axis=1)
    q_pos = PAST_LEN + jnp.arange(t)
    k_pos = jnp.concatenate([PAST_LEN - WINDOW + jnp.arange(WINDOW), q_pos])
    qch = q_pos // CHUNK
    kch = k_pos // CHUNK
    mask = (kch[None, :] <= qch[:, None]) & (kch[None, :] > qch[:, None] - WIN_CHUNKS)
    o = sink_softmax_attention(q, kb, vb, mask, sinks)
    return o.reshape(b, t, A_WIDTH), kb[:, -WINDOW:], vb[:, -WINDOW:]

def hgrn_chunk_step(S, inp):
    q, logf, k, v = inp
    c = q.shape[1]
    cum = jnp.cumsum(logf, axis=1)
    last = cum[:, -1:]
    q_dec = q * jnp.exp(cum)
    k_inv = k * jnp.exp(-cum)
    k_end = k * jnp.exp(last - cum)
    scores = jnp.einsum('bthd,bshd->bhts', q_dec, k_inv)
    causal = jnp.arange(c)[:, None] >= jnp.arange(c)[None, :]
    scores = jnp.where(causal, scores, 0.0)
    o = (jnp.einsum('bhts,bshv->bthv', scores, v)
         + jnp.einsum('bthd,bhdv->bthv', q_dec, S))
    S_new = jnp.exp(last[:, 0])[..., None] * S + jnp.einsum('bshd,bshv->bhdv', k_end, v)
    return S_new, o

def hgrn_prompt(q, logf, k, v):
    b, s = q.shape[:2]
    nc = s // CHUNK

    def to_chunks(a):
        return jnp.moveaxis(a.reshape(b, nc, CHUNK, a.shape[2], a.shape[3]), 1, 0)

    S0 = jnp.zeros((b, B_HEADS, B_KEY_DIM, B_VAL_DIM), jnp.float32)
    S_fin, o = lax.scan(hgrn_chunk_step, S0, (to_chunks(q), to_chunks(logf), to_chunks(k), to_chunks(v)))
    o = jnp.moveaxis(o, 0, 1).reshape(b, s, B_HEADS, B_VAL_DIM)
    return S_fin, o

def mixer_inputs(x, pos, norm_g, w_in, lb):
    bsz, t = x.shape[:2]
    p = rms_norm(x, norm_g) @ w_in
    aq, ak, av, ag, bq, bfg, bi, bg, ma, mb = split_projection(p)
    aq = apply_partial_rope(aq.reshape(bsz, t, A_HEADS, A_HEAD_DIM), pos)
    aq = aq.reshape(bsz, t, A_KV_HEADS, A_GROUP, A_HEAD_DIM)
    ak = apply_partial_rope(ak.reshape(bsz, t, A_KV_HEADS, A_HEAD_DIM), pos)
    av = av.reshape(bsz, t, A_KV_HEADS, A_HEAD_DIM)
    f = lb + (1.0 - lb) * jax.nn.sigmoid(bfg.astype(jnp.float32))
    hs = (bsz, t, B_HEADS, B_KEY_DIM)
    rec = (bq.astype(jnp.float32).reshape(hs), jnp.log(f).reshape(hs), (1.0 - f).reshape(hs),
           bi.astype(jnp.float32).reshape(bsz, t, B_HEADS, B_VAL_DIM))
    return aq, ak, av, ag, rec, bg, ma, mb

def merge_branches(x, attn_o, ag, rec_o, bg, ma, mb, g_norm, w_ba, w_bb, w_o):
    bsz, t = x.shape[:2]
    ya = (attn_o * jax.nn.silu(ag)) @ w_ba
    rn = rec_o * lax.rsqrt(jnp.mean(rec_o * rec_o, axis=-1, keepdims=True) + EPS)
    rn = rn * g_norm.astype(jnp.float32).reshape(B_HEADS, B_VAL_DIM)
    yb = (rn.reshape(bsz, t, B_WIDTH).astype(x.dtype) * jax.nn.silu(bg)) @ w_bb
    merged = jax.nn.sigmoid(ma) * ya + jax.nn.sigmoid(mb) * yb
    return x + merged @ w_o

def setup_inputs(seed: int = 0) -> dict:
    key = jax.random.key(seed)
    ks = jax.random.split(key, 16)
    f32 = jnp.float32
    nrm = jax.random.normal
    return {
        'x_prompt': nrm(ks[0], (BATCH, SEQ, D_MODEL), f32),
        'x_sample': nrm(ks[1], (DEC_BATCH, DEC_SEQ, D_MODEL), f32),
        'cache_attn_k': nrm(ks[2], (DEPTH, DEC_BATCH, WINDOW, A_KV_HEADS, A_HEAD_DIM), f32),
        'cache_attn_v': nrm(ks[3], (DEPTH, DEC_BATCH, WINDOW, A_KV_HEADS, A_HEAD_DIM), f32),
        'state_hgrn': 0.5 * nrm(ks[4], (DEPTH, DEC_BATCH, B_HEADS, B_KEY_DIM, B_VAL_DIM), f32),
        'norm_gain': 1.0 + 0.01 * nrm(ks[5], (DEPTH, D_MODEL), f32),
        'w_in': nrm(ks[6], (DEPTH, D_MODEL, W_IN_COLS), f32) * D_MODEL ** -0.5,
        'attn_sinks': 0.5 * nrm(ks[7], (DEPTH, A_HEADS), f32),
        'hgrn_lb_logits': 0.1 * nrm(ks[8], (DEPTH + 1, B_KEY_WIDTH), f32),
        'hgrn_norm_gain': 1.0 + 0.01 * nrm(ks[9], (DEPTH, B_WIDTH), f32),
        'w_branch_a': nrm(ks[10], (DEPTH, A_WIDTH, D_MODEL), f32) * A_WIDTH ** -0.5,
        'w_branch_b': nrm(ks[11], (DEPTH, B_WIDTH, D_MODEL), f32) * B_WIDTH ** -0.5,
        'w_out': nrm(ks[12], (DEPTH, D_MODEL, D_MODEL), f32) * D_MODEL ** -0.5,
        'final_norm_gain': 1.0 + 0.01 * nrm(ks[13], (D_MODEL,), f32),
    }

def reference(x_prompt, x_sample, cache_attn_k, cache_attn_v, state_hgrn, norm_gain, w_in,
              attn_sinks, hgrn_lb_logits, hgrn_norm_gain, w_branch_a, w_branch_b, w_out,
              final_norm_gain):
    lb_all = jnp.cumsum(jax.nn.softmax(hgrn_lb_logits.astype(jnp.float32), axis=0), axis=0)
    pos_p = jnp.arange(x_prompt.shape[1])
    pos_s = PAST_LEN + jnp.arange(x_sample.shape[1])
    hp = x_prompt
    hs = x_sample
    pk, pv, pS, sk, sv, sS = [], [], [], [], [], []
    for l in range(DEPTH):
        lb = lb_all[l]
        aq, ak, av, ag, rec, bg, ma, mb = mixer_inputs(hp, pos_p, norm_gain[l], w_in[l], lb)
        attn_o = window_attention_prompt(aq, ak, av, attn_sinks[l])
        S_p, rec_o = hgrn_prompt(*rec)
        pk.append(ak[:, -WINDOW:])
        pv.append(av[:, -WINDOW:])
        pS.append(S_p.astype(state_hgrn.dtype))
        hp = merge_branches(hp, attn_o, ag, rec_o, bg, ma, mb, hgrn_norm_gain[l],
                            w_branch_a[l], w_branch_b[l], w_out[l])
        aq, ak, av, ag, rec, bg, ma, mb = mixer_inputs(hs, pos_s, norm_gain[l], w_in[l], lb)
        attn_o, k_buf, v_buf = window_attention_sample(aq, ak, av, cache_attn_k[l], cache_attn_v[l],
                                                       attn_sinks[l])
        S_s, rec_o = hgrn_chunk_step(state_hgrn[l].astype(jnp.float32), rec)
        sk.append(k_buf)
        sv.append(v_buf)
        sS.append(S_s.astype(state_hgrn.dtype))
        hs = merge_branches(hs, attn_o, ag, rec_o, bg, ma, mb, hgrn_norm_gain[l],
                            w_branch_a[l], w_branch_b[l], w_out[l])
    y_prompt = rms_norm(hp, final_norm_gain)
    y_sample = rms_norm(hs, final_norm_gain)
    prompt_attn_k = jnp.stack(pk)
    prompt_attn_v = jnp.stack(pv)
    prompt_hgrn_state = jnp.stack(pS)
    sample_attn_k = jnp.stack(sk)
    sample_attn_v = jnp.stack(sv)
    sample_hgrn_state = jnp.stack(sS)
    return (y_prompt, y_sample, prompt_attn_k, prompt_attn_v, prompt_hgrn_state,
            sample_attn_k, sample_attn_v, sample_hgrn_state)


_drawn_inputs = setup_inputs


def setup_inputs(seed=0):
    import zlib

    import numpy as np

    out = dict(_drawn_inputs(seed))
    spreads = {}
    factors = {'norm_gain': 5.022, 'attn_sinks': 8.0, 'hgrn_norm_gain': 8.0, 'final_norm_gain': 5.483}
    for name, (base, spread) in spreads.items():
        noise = np.random.default_rng([zlib.crc32(name.encode()), seed]).standard_normal(out[name].shape)
        drawn = base * np.exp(spread * noise) if base else spread * noise
        out[name] = __import__('jax').numpy.asarray(drawn.astype(out[name].dtype))
    for name, factor in factors.items():
        out[name] = (out[name] * factor).astype(out[name].dtype)
    return out
```

```python
from contextlib import ExitStack

import concourse.mybir as mybir

F32 = mybir.dt.float32
F32R = mybir.dt.float32r
BF16 = mybir.dt.bfloat16
I32 = mybir.dt.int32
ACT = mybir.ActivationFunctionType
ALU = mybir.AluOpType
AX = mybir.AxisListType

P = 128
D_MODEL = 1024
SEQ, DEC_SEQ = 2048, 64
CHUNK = 64
EPS = 1e-6
NEG_INF = -1e30
WINDOW = 128
HEAD_DIM = 64
A_KV = 2
A_GROUP = 4
ATTN_SCALE = HEAD_DIM ** -0.5
ROPE_DIM = HEAD_DIM // 4
ROPE_THETA = 500000.0
PAST_LEN = 512
B_HEADS = 4

CHUNKS = (SEQ + DEC_SEQ) // CHUNK
GROUPS = 3
NCH = CHUNKS // GROUPS
T = NCH * CHUNK
SUBS = [(0, 6), (6, NCH)]
KT = D_MODEL // P
TILES = [(i * P, min(P, T - i * P)) for i in range((T + P - 1) // P)]
NT = len(TILES)
MERGES = D_MODEL // P
START = 16

BLOCKS = (["ak", "av"] + [f"aq{j}" for j in range(A_GROUP)]
          + [f"{n}{h}" for h in range(B_HEADS) for n in ("bf", "bq", "bi", "bg")]
          + [f"ag{j}" for j in range(A_GROUP)]
          + [f"{n}{j}" for j in range(MERGES) for n in ("ma", "mb", "wab")]
          + [f"wo{hf}{kp}" for hf in range(2) for kp in range(KT // 2)])
NB = len(BLOCKS)
BLOCK = {n: b for b, n in enumerate(BLOCKS)}
SLOTS = 4
SLOT = [b % SLOTS for b in range(NB - SLOTS)] + list(range(SLOTS))


def before(b):
    older = [c for c in range(b) if SLOT[c] == SLOT[b]]
    return (older[-1], 0) if older else (max(c for c in range(NB) if SLOT[c] == SLOT[b]), 1)


def nth_in_slot(b):
    return sum(SLOT[c] == SLOT[b] for c in range(b))


PER_SLOT = [sum(s == k for s in SLOT) for k in range(SLOTS)]


X_STEPS = [("x_square", 0, 0), ("x_sum", 0, 0), ("x_square", 1, 0), ("x_split", 0, 0), ("x_sum", 1, 0),
           ("x_split", 1, 0)]
OUT_BANKS = [3, 4, 5, 0, 1, 2]


def steps(last):
    out = []

    def block(n):
        return [("proj", n, 0), ("proj", n, 1)]

    def hgrn(h):
        return [[("kend_t", h, 0), ("kend_t", h, 1), ("scores_b", h, 0), ("scores_b", h, 1)],
                [("v_t", h, 0), ("v_t", h, 1)],
                [],
                [("update", h, r) for r in range(4)],
                [],
                [("read_out", h, 0), ("read_out", h, 1)],
                [("sum_sq", h, 0), ("sum_sq", h, 1)],
                [("finish", h, 0)]]

    for n in ["ak", "av", "aq0", "aq1"]:
        out += block(n)
    out += [("v_win", r, 0) for r in range(3)] + [("k_win", 0, 0)]
    for n in ["aq2", "aq3"]:
        out += block(n)
    heads = [s for h in range(B_HEADS) for n in ("bf", "bq", "bi", "bg") for s in block(f"{n}{h}")]
    for n, s in enumerate(heads):
        out.append(s)
        k = (n - 2) // 2
        even = [("probs_t", k - 2, 0), ("scores", k, 0), ("normalise", k - 1, 0)]
        odd = [("softmax", k, 0), ("attend", k - 2, 0)]
        ahead, after = ([], even) if n % 2 == 0 else (odd[:1], odd[1:])
        if n >= 8:
            ahead = ahead + hgrn(n // 8 - 1)[n % 8]
        out += [t for t in ahead + after if t[0] not in ("probs_t", "scores", "normalise", "softmax", "attend")
                or 0 <= t[1] < NCH]
    gates = [s for j in range(A_GROUP) for s in block(f"ag{j}")]
    for n, s in enumerate(gates):
        out.append(s)
        out += hgrn(B_HEADS - 1)[n]
    for j in range(MERGES):
        out += [(n, j, s) for n in ("ma", "mb", "ya", "yb") for s in range(2)]
    prepare = {0: X_STEPS[0:1], 1: X_STEPS[1:3], 2: X_STEPS[3:5], 4: X_STEPS[5:6]}
    for p in range(KT):
        out.append(("out", p // 4, p % 4))
        if not last:
            out += prepare.get(p, [])
    return out


def banks(step):
    kind, a, b = step
    return {"v_win": [7 - a], "k_win": [4], "scores": [3, 4], "probs_t": [5], "attend": [6],
            "kend_t": [7 - b], "v_t": [7 - b], "scores_b": [3 + b], "update": [[3, 4, 5, 7][b]],
            "read_out": [7 - b], "sum_sq": [3 + b], "x_sum": [6 + a]}.get(kind, [])


def plan(last):
    count, use, proj = [0] * 8, {}, 0
    place = {}
    for s in steps(last):
        if s[0] in ("proj", "ma", "mb", "ya", "yb"):
            bs, proj = [proj % 3], proj + 1
        elif s[0] == "out":
            bs = OUT_BANKS if s[2] == 0 else []
        else:
            bs = banks(s)
        place[s] = bs
        for b in bs:
            use[s, b] = count[b]
            count[b] += 1
    return use, place, count


PLAN = {last: plan(last) for last in (False, True)}
USES = PLAN[False][2]
PRIOR = [1 if b in (6, 7) else 0 for b in range(8)]
UPDATES = [[0, 2, 4, 6], [1, 3, 5, 7], [8, 10], [9]]


def program(nc, x, x_t, w, cache_k, cache_v, state, norm_gain, sinks, lb_logits, hgrn_gain, final_gain,
            rope_cos, rope_sin, causal, identity, first_mask, keep_state,
            y, win_k, win_v, state_first, state_last):
    ctx = ExitStack()
    base = (nc.sbuf_base + 31) // 32 * 32
    top = [base]

    def sb(name, shape, dt=F32, at=None):
        size = 2 if dt == BF16 else 4
        for n in shape[1:]:
            size *= n
        size = (size + 31) // 32 * 32
        if at is None:
            at = top[0]
            top[0] += size
        return nc.alloc_sbuf_tensor_at(name, shape, dt, offset=at), at, at + size

    def own(name, shape, dt=F32, at=None):
        return sb(name, shape, dt, at)[0]

    x_hi = own("x_hi", [P, KT, T], F32R)
    x_lo, at_x_lo, _ = sb("x_lo", [P, KT, T], F32R)
    x_raw = own("x_raw", [P, KT, T], F32, at_x_lo)
    ga_hi, at_ga_hi, _ = sb("ga_hi", [P, NCH, A_GROUP, CHUNK], F32R)
    gb_hi, at_gb_hi, _ = sb("gb_hi", [P, B_HEADS, T], F32R)
    ga_lo, at_ga_lo, _ = sb("ga_lo", [P, NCH, A_GROUP, CHUNK], F32R)
    gb_lo, at_gb_lo, _ = sb("gb_lo", [P, B_HEADS, T], F32R)
    q_rot = own("q_rot", [P, NCH, A_GROUP, CHUNK], F32, at_ga_hi)
    attn_o = own("attn_o", [P, NCH, A_GROUP, CHUNK], F32, at_ga_lo)
    q_dec = own("q_dec", [P, B_HEADS, T], F32, at_gb_hi)
    gate_b = own("gate_b", [P, B_HEADS, T], F32, at_gb_lo)
    res = own("res", [P, NT, D_MODEL], F32, at_ga_hi)
    w_hi, w_lo, w_raw = [], [], []
    for s in range(SLOTS):
        w_hi.append(own(f"w_hi{s}", [P, KT, P], F32R))
        t, at, _ = sb(f"w_lo{s}", [P, KT, P], F32R)
        w_lo.append(t)
        w_raw.append(own(f"w_raw{s}", [P, KT, P], F32, at))
    fgain = own("fgain", [P, D_MODEL])
    ident, ones = own("ident", [P, P]), own("ones", [P, P])
    caus = own("caus", [P, P], I32)
    start_f = own("start_f", [P, T])
    end_one = own("end_one", [P, T], BF16)
    carry_s = own("carry_s", [P, B_HEADS, P])
    carry_k, carry_v = own("carry_k", [P, CHUNK]), own("carry_v", [P, CHUNK])
    s_first = own("s_first", [P, P])
    decay = own("decay", [P, B_HEADS, NCH])
    gain, gain_b = own("gain", [P, KT]), own("gain_b", [P, B_HEADS])
    sink, neg_sink = own("sink", [P, 4]), own("neg_sink", [P, 4])
    lb, one_lb, logit = own("lb", [P, 4]), own("one_lb", [P, 4]), own("logit", [P, 2, 4])
    eps, pad = own("eps", [P, 1]), own("pad", [P, 1])
    amask, keep = own("amask", [P, 1]), own("keep", [P, 1], I32)
    rmax, nmax, sarg = own("rmax", [P, 2, 4]), own("nmax", [P, 2, 4]), own("sarg", [P, 2, 4])
    psum_, esink, rden = own("psum_", [P, 2, 4]), own("esink", [P, 2, 4]), own("rden", [P, 2, 4])
    yss = own("yss", [P, NT])
    region = top[0]
    f, _, _ = sb("f", [P, T + 1])
    prod, rev, inv = own("prod", [P, T]), own("rev", [P, T]), own("inv", [P, T])
    keyb = own("keyb", [P, T])
    vb = own("vb", [P, T])
    kend_tok, v_tok, sc_t = own("kend_tok", [P, NT, P]), own("v_tok", [P, NT, P]), own("sc_t", [P, NT, P])
    st = own("st", [P, NCH, P])
    sq, rs, ob = own("sq", [P, T]), own("rs", [P, T]), own("ob", [P, T])
    merged_bytes = 2 * MERGES * T * 4
    assert top[0] - region <= merged_bytes, (top[0] - region, merged_bytes)
    top[0] = region + merged_bytes
    m_hi = own("m_hi", [P, MERGES, T], F32R, region)
    m_lo = own("m_lo", [P, MERGES, T], F32R, region + merged_bytes // 2)
    attn_at = top[0]
    k_rot, v_t = own("k_rot", [P, T + CHUNK]), own("v_t", [P, T + CHUNK])
    v_win = own("v_win", [P, NCH, P])
    probs = own("probs", [P, 2, 4, P])
    probs_t = own("probs_t", [P, 4, P])
    k_win = own("k_win", [P, 2, P])
    swap, raw = own("swap", [P, T]), own("raw", [P, T])
    attn_end = top[0]
    top[0] = attn_at
    sig_a, sig_b = own("sig_a", [P, T]), own("sig_b", [P, T])
    scratch = own("scratch", [P, D_MODEL])
    x_acc = own("x_acc", [P, 2, 2, SUBS[0][1] * CHUNK])
    x_sq = own("x_sq", [P, 2, 2, SUBS[0][1] * CHUNK])
    assert top[0] <= attn_end, (top[0], attn_end)
    top[0] = attn_end
    cos, sin = own("cos", [P, T]), own("sin", [P, T])
    assert top[0] <= nc.sbuf_usable_end, (top[0], nc.sbuf_usable_end)

    pb = [nc.alloc_psum_tensor(f"bank{b}", [P, 512], F32) for b in range(8)]

    full = [nc.alloc_semaphore(f"bank{b}_full") for b in range(8)]
    read = [nc.alloc_semaphore(f"bank{b}_read") for b in range(8)]
    sem = nc.alloc_semaphore
    w_landed = [sem(f"w_landed{s}") for s in range(SLOTS)]
    w_high, w_split = sem("w_high"), sem("w_split")
    piece_used = sem("piece_used")
    consts_in, consts_made = sem("consts_in"), sem("consts_made")
    lb_max, lb_exp, lb_made = sem("lb_max"), sem("lb_exp"), sem("lb_made")
    rope_in, flags_in = sem("rope_in"), sem("flags_in")
    k_roped, q_roped, raw_free = sem("k_roped"), sem("q_roped"), sem("raw_free")
    windows_out = sem("windows_out")
    carried = sem("carried")
    row_max, probs_exp, probs_norm = sem("row_max"), sem("probs_exp"), sem("probs_norm")
    f_used, keys_made = sem("f_used"), sem("keys_made")
    sig_made = sem("sig_made")
    first_made, first_out, last_made, last_out = (sem("first_made"), sem("first_out"),
                                                  sem("last_made"), sem("last_out"))
    ob_copied, finished, gated_a = sem("ob_copied"), sem("finished"), sem("gated_a")
    merged = sem("merged")
    x_landed = [[sem(f"x_landed{s}{q}") for q in range(4)] for s in range(2)]
    x_squared, x_added, x_summed = sem("x_squared"), sem("x_added"), sem("x_summed")
    x_scaled, x_high, x_split = sem("x_scaled"), sem("x_high"), sem("x_split")
    gain_in = sem("gain_in")
    res_in = [sem(f"res_in{i}") for i in range(NT)]
    summed, y_root, y_made, y_out = sem("summed"), sem("y_root"), sem("y_made"), sem("y_out")
    act_step, dve_step = sem("act_step"), sem("dve_step")

    def use(g, last, step, b):
        if g is None:
            return 0
        return PRIOR[b] + USES[b] * g + PLAN[last][0][step, b]

    def wait_full(eng, g, last, step, b):
        eng.wait_ge(full[b], use(g, last, step, b) + 1)

    def wait_read(eng, g, last, step, b):
        eng.wait_ge(read[b], START + use(g, last, step, b) + 1)

    def wait_bank_free(eng, g, last, step, b):
        eng.wait_ge(read[b], START + use(g, last, step, b))

    def bank_of(last, step):
        return PLAN[last][1][step][0]

    def sub(s):
        return SUBS[s][0] * CHUNK, SUBS[s][1] * CHUNK

    def last_step_of(b):
        n = BLOCKS[b]
        if n.startswith("wab"):
            return ("yb", int(n[3:]), 1)
        if n[:2] in ("ma", "mb"):
            return (n[:2], int(n[2:]), 1)
        return ("proj", n, 1)

    def groups(eng, body):
        with eng.Fori(0, GROUPS - 1) as g:
            body(g, False)
        body(GROUPS - 1, True)

    block = ctx.enter_context(nc.Block())

    @block.sync
    def _(sp):
        def load_block(g, b, slots_wait, last=False):
            if slots_wait:
                c, back = before(b)
                gg = g - back
                if BLOCKS[c].startswith("wo"):
                    hf, kp = int(BLOCKS[c][2]), int(BLOCKS[c][3])
                    sp.wait_ge(piece_used, 8 * gg + 4 * hf + kp + 1)
                else:
                    s = last_step_of(c)
                    wait_full(sp, gg, last, s, bank_of(last, s))
            sp.dma_start(w_raw[SLOT[b]][:], w[b]).then_inc(w_landed[SLOT[b]], 16)

        def fetch_x(g, s):
            lo, hi = sub(s)
            for q in range(4):
                k = slice(2 * q, 2 * q + 2)
                sp.dma_start(x_raw[:, k, lo:hi], x_t[g, :, k, lo:hi]).then_inc(x_landed[s][q], 16)

        fetch_x(0, 0)
        load_block(0, 0, False)
        load_block(0, 1, False)
        fetch_x(0, 1)
        load_block(0, 2, False)
        load_block(0, 3, False)

        def body(g, last):
            sp.wait_ge(q_roped, START + A_GROUP * g)
            sp.dma_start(cos[:], rope_cos[g]).then_inc(rope_in, 16)
            sp.dma_start(sin[:], rope_sin[g]).then_inc(rope_in, 16)
            sp.wait_ge(row_max, START + NCH * g)
            sp.dma_start(amask[:], first_mask[g]).then_inc(flags_in, 16)
            sp.wait_ge(last_made, START + B_HEADS * g)
            sp.dma_start(keep[:], keep_state[g]).then_inc(flags_in, 16)
            for b in range(SLOTS, NB):
                load_block(g, b, True, last)
                if b == NB - 6 and not last:
                    s = ("mb", MERGES - 1, 1)
                    wait_full(sp, g, last, s, bank_of(last, s))
                    fetch_x(g + 1, 0)
                if b == NB - 4 and not last:
                    fetch_x(g + 1, 1)
                if b == NB - 5:
                    s = ("yb", MERGES - 1, 1)
                    wait_full(sp, g, last, s, bank_of(last, s))
                    for i, (t0, n) in enumerate(TILES):
                        sp.dma_start(res[0:n, i, :], x[g, t0:t0 + n, :]).then_inc(res_in[i], 16)
            if not last:
                for b in range(SLOTS):
                    load_block(g + 1, b, True)
            for i, (t0, n) in enumerate(TILES):
                sp.wait_ge(y_made, NT * g + i + 1)
                sp.dma_start(y[g, t0:t0 + n, :], res[0:n, i, :]).then_inc(y_out, 16)

        groups(sp, body)
        sp.wait_ge(y_out, START + 16 * NT * GROUPS)
        sp.wait_ge(windows_out, 16 * 4 * GROUPS)
        sp.wait_ge(first_out, START + 16 * B_HEADS * GROUPS)
        sp.wait_ge(last_out, START + 16 * B_HEADS * GROUPS)

    @block.gpsimd
    def _(pool):
        for signal in (*read, raw_free, f_used, finished, merged, gated_a, first_out, last_out, y_out,
                       row_max, q_roped, last_made):
            pool.sem_inc(signal, START)

        def body(g, last):
            for b in range(NB):
                s = SLOT[b]
                pool.wait_ge(w_high, NB * g + b + 1)
                pool.tensor_tensor(w_lo[s][:], w_raw[s][:], w_hi[s][:].bitcast(F32),
                                   ALU.subtract).then_inc(w_split, 1)

        groups(pool, body)

    @block.scalar
    def _(act):
        links = [0]

        def link(ins):
            links[0] += 1
            ins.then_inc(act_step, 1)
            act.wait_ge(act_step, links[0])

        def high(g, b):
            s = SLOT[b]
            act.wait_ge(w_landed[s], 16 * (PER_SLOT[s] * g + nth_in_slot(b) + 1))
            act.activation(w_hi[s][:], w_raw[s][:], ACT.Copy).then_inc(w_high, 1)

        def prepare_x(step, g, gn, last):
            kind, s, _ = step
            lo, hi = sub(s)
            n = hi - lo
            if kind == "x_square":
                for q in range(4):
                    act.wait_ge(x_landed[s][q], 16 * (gn + 1))
                    dst = x_acc[:, s, :, 0:n]
                    if q:
                        k = 3 * s + q - 1
                        dst = x_sq[:, k % 2, :, 0:n]
                        if g is not None or k >= 2:
                            act.wait_ge(x_added, 6 * gn + k - 1)
                    act.activation(dst, x_raw[:, 2 * q:2 * q + 2, lo:hi], ACT.Square).then_inc(x_squared, 1)
            elif kind == "x_sum":
                b = 6 + s
                wait_full(act, g, last, step, b)
                act.activation(x_acc[:, s, 1, 0:n], pb[b][:, 0:n], ACT.Sqrt, scale=1.0 / D_MODEL,
                               bias=eps[:]).then_inc(read[b], 1)
            else:
                for q in range(4):
                    k = slice(2 * q, 2 * q + 2)
                    act.wait_ge(x_scaled, 8 * gn + 4 * s + q + 1)
                    act.activation(x_hi[:, k, lo:hi], x_raw[:, k, lo:hi], ACT.Copy).then_inc(x_high, 1)

        act.dma_start(gain[:], norm_gain).then_inc(gain_in, 16)
        for t, a in ((ident, identity), (caus, causal), (gain_b, hgrn_gain), (sink, sinks),
                     (logit, lb_logits), (carry_k, cache_k), (carry_v, cache_v), (carry_s, state),
                     (fgain, final_gain)):
            act.dma_start(t[:], a).then_inc(consts_in, 16)
        act.wait_ge(consts_made, 1)
        for step in X_STEPS:
            prepare_x(step, None, 0, False)
            if step == ("x_square", 0, 0):
                high(0, 0)
            if step == ("x_square", 1, 0):
                high(0, 1)
        act.wait_ge(lb_max, 1)
        act.activation(logit[:], logit[:], ACT.Exp).then_inc(lb_exp, 1)

        def body(g, last):
            act.sem_clear(act_step)
            links[0] = 0
            seen = set()

            def ahead(n):
                b = BLOCK[n]
                if b in seen:
                    return
                seen.add(b)
                if b + 2 < NB:
                    high(g, b + 2)
                elif not last:
                    high(g + 1, b + 2 - NB)

            for step in steps(last):
                kind, a, s = step
                if kind == "proj":
                    ahead(a)
                    bank = bank_of(last, step)
                    lo, hi = sub(s)
                    src = pb[bank][:, 0:hi - lo]
                    n = a[:2]
                    if n in ("ak", "aq"):
                        i = 0 if n == "ak" else 1 + int(a[2:])
                        wait_full(act, g, last, step, bank)
                        if s == 0:
                            act.wait_ge(raw_free, START + 5 * g + i)
                            if n == "ak":
                                act.wait_ge(gated_a, START + 2 * A_GROUP * g)
                        act.activation(raw[:, lo:hi], src, ACT.Copy).then_inc(read[bank], 1)
                    elif n == "av":
                        wait_full(act, g, last, step, bank)
                        act.activation(v_t[:, CHUNK + lo:CHUNK + hi], src, ACT.Copy).then_inc(read[bank], 1)
                    elif n == "bf":
                        h = int(a[2:])
                        wait_full(act, g, last, step, bank)
                        act.wait_ge(f_used, START + B_HEADS * g + h)
                        act.activation(f[:, lo:hi], src, ACT.Sigmoid).then_inc(read[bank], 1)
                    elif n == "bi":
                        wait_full(act, g, last, step, bank)
                        act.activation(vb[:, lo:hi], src, ACT.Copy).then_inc(read[bank], 1)
                    elif n == "bg":
                        h = int(a[2:])
                        wait_full(act, g, last, step, bank)
                        act.activation(gate_b[:, h, lo:hi], src, ACT.Sigmoid).then_inc(sig_made, 1)
                    elif n == "ag":
                        j = int(a[2:])
                        wait_full(act, g, last, step, bank)
                        if j:
                            act.wait_ge(gated_a, START + 2 * A_GROUP * g + 2 * j + s - 1)
                        else:
                            act.wait_ge(raw_free, START + 5 * (g + 1))
                        act.activation(raw[:, lo:hi], src, ACT.Sigmoid).then_inc(sig_made, 1)
                elif kind == "v_win":
                    cs = range(4 * a, min(4 * a + 4, NCH))
                    b = banks(step)[0]
                    wait_full(act, g, last, step, b)
                    act.activation(v_win[:, cs[0]:cs[-1] + 1, :], pb[b][:, 0:P * len(cs)].rearrange(
                        "p (c d) -> p c d", d=P), ACT.Copy).then_inc(read[b], 1)
                elif kind == "k_win":
                    wait_full(act, g, last, step, 4)
                    act.activation(k_win[:], pb[4][:, 0:2 * P].rearrange("p (c d) -> p c d", d=P),
                                   ACT.Copy).then_inc(read[4], 1)
                    wait_read(act, g, last, step, 4)
                    wait_read(act, g, last, ("v_win", 2, 0), 5)
                    for i, c in enumerate((0, NCH - 1)):
                        act.dma_start(win_k[g, i], k_win[:, i, :]).then_inc(windows_out, 16)
                        act.dma_start(win_v[g, i], v_win[:, c, :]).then_inc(windows_out, 16)
                elif kind == "softmax":
                    c = a
                    k = c % 2
                    act.wait_ge(row_max, START + NCH * g + c + 1)
                    if c >= 2:
                        wait_full(act, g, last, ("probs_t", c - 2, 0), 5)
                    for i in range(4):
                        e = act.activation(probs[:, k, i, :], pb[3 + i // 2][:, (i % 2) * P:(i % 2 + 1) * P],
                                           ACT.Exp, scale=ATTN_SCALE, bias=nmax[:, k, i:i + 1],
                                           accum_out=psum_[:, k, i:i + 1])
                        if i % 2:
                            e.then_inc(read[3 + i // 2], 1)
                    act.activation(esink[:, k, :], sarg[:, k, :], ACT.Exp).then_inc(probs_exp, 1)
                elif kind == "probs_t":
                    wait_full(act, g, last, step, 5)
                    if a >= 1:
                        wait_full(act, g, last, ("attend", a - 1, 0), 6)
                    act.activation(probs_t[:], pb[5][:].rearrange("p (i q) -> p i q", i=4),
                                   ACT.Copy).then_inc(read[5], 1)
                elif kind == "attend":
                    wait_full(act, g, last, step, 6)
                    act.activation(attn_o[:, a, :, :], pb[6][:, 0:A_GROUP * CHUNK].rearrange(
                        "p (j q) -> p j q", j=A_GROUP), ACT.Copy).then_inc(read[6], 1)
                elif kind in ("kend_t", "v_t"):
                    b = banks(step)[0]
                    dst = kend_tok if kind == "kend_t" else v_tok
                    wait_full(act, g, last, step, b)
                    if s == 0:
                        act.activation(dst[:, 0:4, :], pb[b][:].rearrange("p (i d) -> p i d", i=4),
                                       ACT.Copy).then_inc(read[b], 1)
                    else:
                        act.activation(dst[:, 4, :], pb[b][:, 0:P], ACT.Copy)
                        act.activation(dst[0:CHUNK, 5, :], pb[b][0:CHUNK, P:2 * P],
                                       ACT.Copy).then_inc(read[b], 1)
                elif kind == "read_out":
                    b = banks(step)[0]
                    lo, hi = (0, 512) if s == 0 else (512, T)
                    if s == 0:
                        act.wait_ge(first_made, B_HEADS * g + a + 1)
                        act.dma_start(state_first[g, a], s_first[:]).then_inc(first_out, 16)
                        act.wait_ge(last_made, START + B_HEADS * g + a + 1)
                        act.dma_start(state_last[g, a], carry_s[:, a, :]).then_inc(last_out, 16)
                    wait_full(act, g, last, step, b)
                    act.wait_ge(finished, START + B_HEADS * g + a)
                    act.activation(ob[:, lo:hi], pb[b][:, 0:hi - lo], ACT.Copy).then_inc(ob_copied, 1)
                    act.activation(sq[:, lo:hi], pb[b][:, 0:hi - lo], ACT.Square).then_inc(read[b], 1)
                elif kind == "sum_sq":
                    b = banks(step)[0]
                    lo, hi = (0, 512) if s == 0 else (512, T)
                    wait_full(act, g, last, step, b)
                    act.activation(rs[:, lo:hi], pb[b][:, 0:hi - lo], ACT.Sqrt, scale=1.0 / P,
                                   bias=eps[:]).then_inc(read[b], 1)
                elif kind in ("ma", "mb"):
                    ahead(f"{kind}{a}")
                    bank = bank_of(last, step)
                    lo, hi = sub(s)
                    dst = sig_a if kind == "ma" else sig_b
                    wait_full(act, g, last, step, bank)
                    if kind == "ma" and s == 0:
                        act.wait_ge(merged, START + 2 * MERGES * g + 2 * a)
                        if a == 0:
                            act.wait_ge(windows_out, 16 * 4 * (g + 1))
                    act.activation(dst[:, lo:hi], pb[bank][:, 0:hi - lo], ACT.Sigmoid).then_inc(read[bank], 1)
                elif kind == "ya":
                    ahead(f"wab{a}")
                elif kind == "out":
                    ahead(f"wo{a}{s}")
                elif kind.startswith("x_"):
                    prepare_x(step, g, g + 1, last)
            for i, (t0, n) in enumerate(TILES):
                act.wait_ge(summed, NT * g + i + 1)
                link(act.activation(scratch[0:n, :], res[0:n, i, :], ACT.Square,
                                    accum_out=yss[0:n, i:i + 1]))
                act.activation(yss[0:n, i:i + 1], yss[0:n, i:i + 1], ACT.Sqrt, scale=1.0 / D_MODEL,
                               bias=eps[0:n, :]).then_inc(y_root, 1)

        groups(act, body)

    @block.vector
    def _(dve):
        links = [0]

        def link(ins):
            links[0] += 1
            ins.then_inc(dve_step, 1)
            dve.wait_ge(dve_step, links[0])

        def prepare_x(step, g, gn, last):
            kind, s, _ = step
            lo, hi = sub(s)
            n = hi - lo
            if kind == "x_square":
                dve.wait_ge(x_squared, 8 * gn + 4 * s + 1)
                for q in range(1, 4):
                    k = 3 * s + q - 1
                    dve.wait_ge(x_squared, 8 * gn + 4 * s + q + 1)
                    v = x_acc[:, s, :, 0:n]
                    dve.tensor_tensor(v, v, x_sq[:, k % 2, :, 0:n], ALU.add).then_inc(x_added, 1)
                    dve.wait_ge(x_added, 6 * gn + k + 1)
                dve.tensor_tensor(x_acc[:, s, 0, 0:n], x_acc[:, s, 0, 0:n], x_acc[:, s, 1, 0:n],
                                  ALU.add).then_inc(x_summed, 1)
            elif kind == "x_split":
                rms = x_acc[:, s, 1, 0:n]
                wait_read(dve, g, last, ("x_sum", s, 0), 6 + s)
                link(dve.reciprocal(rms, rms))

                def low(q):
                    k = slice(2 * q, 2 * q + 2)
                    dve.wait_ge(x_high, 8 * gn + 4 * s + q + 1)
                    return dve.tensor_tensor(x_lo[:, k, lo:hi], x_raw[:, k, lo:hi],
                                             x_hi[:, k, lo:hi].bitcast(F32), ALU.subtract)

                for q in range(4):
                    for kt in (2 * q, 2 * q + 1):
                        v = x_raw[:, kt, lo:hi]
                        ins = dve.scalar_tensor_tensor(out=v, in0=v, scalar=gain[:, kt:kt + 1], in1=rms,
                                                       op0=ALU.mult, op1=ALU.mult)
                    ins.then_inc(x_scaled, 1)
                    if q:
                        low(q - 1)
                low(3).then_inc(x_split, 1)

        dve.memset(eps[:], EPS)
        dve.memset(ones[:], 1.0)
        dve.memset(start_f[:], 0.0)
        link(dve.memset(end_one[:], 0.0))
        dve.memset(end_one[:, CHUNK - 1:T:CHUNK], 1.0).then_inc(consts_made, 1)
        dve.wait_ge(consts_made, 1)
        dve.wait_ge(gain_in, 16)
        for step in X_STEPS:
            prepare_x(step, None, 0, False)
        dve.wait_ge(consts_in, 16 * 9)
        link(dve.tensor_scalar(neg_sink[:], sink[:], -1.0, None, ALU.mult))
        link(dve.tensor_tensor(lb[:], logit[:, 0, :], logit[:, 1, :], ALU.max))
        dve.tensor_tensor(logit[:], logit[:], lb[:, None, :].broadcast_to([P, 2, 4]),
                          ALU.subtract).then_inc(lb_max, 1)
        dve.wait_ge(lb_exp, 1)
        link(dve.tensor_tensor(lb[:], logit[:, 0, :], logit[:, 1, :], ALU.add))
        link(dve.reciprocal(lb[:], lb[:]))
        link(dve.tensor_tensor(lb[:], lb[:], logit[:, 0, :], ALU.mult))
        link(dve.tensor_scalar(one_lb[:], lb[:], -1.0, 1.0, ALU.mult, ALU.add))

        def split(hi, lo, val):
            link(dve.tensor_copy(hi, val))
            return dve.tensor_tensor(lo, val, hi.bitcast(F32), ALU.subtract)

        def final_norm(g, i):
            n = TILES[i][1]
            dve.wait_ge(y_root, NT * g + i + 1)
            link(dve.reciprocal(yss[0:n, i:i + 1], yss[0:n, i:i + 1]))
            dve.scalar_tensor_tensor(out=res[0:n, i, :], in0=res[0:n, i, :], scalar=yss[0:n, i:i + 1],
                                     in1=fgain[0:n, :], op0=ALU.mult, op1=ALU.mult).then_inc(y_made, 1)

        def rotate(dst, first):
            v = "p (c t) -> p c t"
            link(dve.tensor_tensor(dst, raw[:].rearrange(v, t=CHUNK), cos[:].rearrange(v, t=CHUNK), ALU.mult))
            link(dve.stream_shuffle(swap[:], raw[:], [i ^ (ROPE_DIM // 2) for i in range(32)]))
            dve.tensor_tensor(swap[:], swap[:], sin[:], ALU.mult).then_inc(raw_free, 1)
            dve.wait_ge(raw_free, START + first)
            return dve.tensor_tensor(dst, dst, swap[:].rearrange(v, t=CHUNK), ALU.add)

        def body(g, last):
            dve.sem_clear(dve_step)
            links[0] = 0
            for step in steps(last):
                kind, a, s = step
                if kind == "proj":
                    bank = bank_of(last, step)
                    lo, hi = sub(s)
                    src = pb[bank][:, 0:hi - lo]
                    n = a[:2]
                    if n == "ak" and s == 1:
                        for r in range(2):
                            wait_read(dve, g, last, ("proj", a, r), bank_of(last, ("proj", a, r)))
                        dve.wait_ge(rope_in, 32 * (g + 1))
                        link(dve.tensor_copy(k_rot[:, 0:CHUNK], carry_k[:]))
                        k = k_rot[:, CHUNK:].rearrange("p (c t) -> p c t", t=CHUNK)
                        link(rotate(k, 5 * g + 1))
                        dve.tensor_copy(carry_k[:], k_rot[:, T:T + CHUNK]).then_inc(k_roped, 1)
                        link(dve.tensor_copy(v_t[:, 0:CHUNK], carry_v[:]))
                        dve.sem_inc(carried, 1)
                    elif n == "av" and s == 1:
                        wait_read(dve, g, last, step, bank)
                        link(dve.tensor_copy(carry_v[:], v_t[:, T:T + CHUNK]))
                    elif n == "aq" and s == 1:
                        j = int(a[2:])
                        for r in range(2):
                            wait_read(dve, g, last, ("proj", a, r), bank_of(last, ("proj", a, r)))
                        if j == 0:
                            dve.wait_ge(y_out, START + 16 * NT * g)
                        rotate(q_rot[:, :, j, :], 5 * g + 2 + j).then_inc(q_roped, 1)
                        dve.wait_ge(q_roped, START + A_GROUP * g + j + 1)
                    elif n == "bf" and s == 1:
                        h = int(a[2:])
                        for r in range(2):
                            wait_read(dve, g, last, ("proj", a, r), bank_of(last, ("proj", a, r)))
                        link(dve.tensor_scalar(f[:, 0:T], f[:, 0:T], one_lb[:, h:h + 1], lb[:, h:h + 1],
                                               ALU.mult, ALU.add))
                        dve.tensor_scalar(keyb[:], f[:, 0:T], -1.0, 1.0, ALU.mult, ALU.add)
                        link(dve.tensor_copy(start_f[:, 0:T:CHUNK], f[:, 0:T:CHUNK]))
                        link(dve.memset(f[:, 0:T + 1:CHUNK], 0.0))
                        link(dve.tensor_tensor_scan(prod[:], f[:, 0:T], start_f[:], 0.0, ALU.mult, ALU.add))
                        if h:
                            wait_full(dve, g, last, ("kend_t", h - 1, 1), 6)
                            wait_full(dve, g, last, ("scores_b", h - 1, 1), 4)
                        dve.tensor_tensor_scan(rev[:, ::-1], f[:, T:0:-1], end_one[:, ::-1],
                                               0.0, ALU.mult, ALU.add).then_inc(f_used, 1)
                        link(dve.tensor_copy(decay[:, h, :], prod[:, CHUNK - 1:T:CHUNK]))
                        link(dve.reciprocal(inv[:], prod[:]))
                        dve.wait_ge(f_used, START + B_HEADS * g + h + 1)
                        link(dve.tensor_tensor(inv[:], inv[:], keyb[:], ALU.mult))
                        link(dve.tensor_tensor(rev[:], rev[:], keyb[:], ALU.mult))
                        dve.sem_inc(keys_made, 1)
                    elif n == "bq":
                        h = int(a[2:])
                        wait_full(dve, g, last, step, bank)
                        dve.tensor_tensor(q_dec[:, h, lo:hi], src, prod[:, lo:hi], ALU.mult).then_inc(read[bank], 1)
                    elif n == "bg":
                        h = int(a[2:])
                        dve.wait_ge(sig_made, 16 * g + 2 * h + s + 1)
                        dve.tensor_tensor(gate_b[:, h, lo:hi], src, gate_b[:, h, lo:hi],
                                          ALU.mult).then_inc(read[bank], 1)
                    elif n == "ag":
                        j = int(a[2:])
                        c0, c1 = SUBS[s]
                        dve.wait_ge(sig_made, 16 * g + 2 * (B_HEADS + j) + s + 1)
                        v = raw[:, lo:hi]
                        dve.tensor_tensor(v, src, v, ALU.mult).then_inc(read[bank], 1)
                        wait_read(dve, g, last, step, bank)
                        vv = v.rearrange("p (c t) -> p c t", t=CHUNK)
                        if j == 0 and s == 0:
                            wait_read(dve, g, last, ("attend", NCH - 1, 0), 6)
                        link(dve.tensor_tensor(vv, vv, attn_o[:, c0:c1, j, :], ALU.mult))
                        split(ga_hi[:, c0:c1, j, :], ga_lo[:, c0:c1, j, :], vv).then_inc(gated_a, 1)
                elif kind == "scores":
                    c, k = a, a % 2
                    wait_full(dve, g, last, step, 3)
                    wait_full(dve, g, last, step, 4)
                    if c >= 2:
                        dve.wait_ge(probs_exp, NCH * g + c - 1)
                    if c == 1:
                        dve.wait_ge(flags_in, 32 * (g + 1))
                        for b in (3, 4):
                            v = pb[b][:, 0:2 * P].rearrange("p (i k) -> p i k", i=2)[:, :, 0:CHUNK]
                            link(dve.tensor_scalar(v, v, amask[:, 0:1], None, ALU.add))
                    for b in (3, 4):
                        link(dve.tensor_reduce(rmax[:, k, 2 * (b - 3):2 * (b - 3) + 2],
                                               pb[b][:, 0:2 * P].rearrange("p (i k) -> p i k", i=2),
                                               AX.X, ALU.max))
                    link(dve.scalar_tensor_tensor(out=nmax[:, k, :], in0=rmax[:, k, :], scalar=-ATTN_SCALE,
                                                  in1=neg_sink[:], op0=ALU.mult, op1=ALU.min))
                    dve.tensor_tensor(sarg[:, k, :], sink[:], nmax[:, k, :], ALU.add).then_inc(row_max, 1)
                elif kind == "normalise":
                    c, k = a, a % 2
                    dve.wait_ge(probs_exp, NCH * g + c + 1)
                    link(dve.tensor_tensor(rden[:, k, :], psum_[:, k, :], esink[:, k, :], ALU.add))
                    link(dve.reciprocal(rden[:, k, :], rden[:, k, :]))
                    dve.tensor_tensor(probs[:, k, :, :], probs[:, k, :, :],
                                      rden[:, k, :, None].broadcast_to([P, 4, P]),
                                      ALU.mult).then_inc(probs_norm, 1)
                elif kind == "scores_b":
                    h, b = a, banks(step)[0]
                    if h == 0 and s == 0:
                        wait_full(dve, g, last, step, b)
                        link(dve.memset(sc_t[:], 0.0))
                    if h and s == 0:
                        wait_full(dve, g, last, ("read_out", h - 1, 1), 6)
                    wait_full(dve, g, last, step, b)
                    link(dve.memset(pad[:], 0.0))
                    if s == 0:
                        dve.copy_predicated(sc_t[:, 0:4, :], caus[:, None, :].broadcast_to([P, 4, P]),
                                            pb[b][:].rearrange("p (i t) -> p i t", i=4)).then_inc(read[b], 1)
                    else:
                        dve.copy_predicated(sc_t[:, 4, :], caus[:], pb[b][:, 0:P])
                        dve.copy_predicated(sc_t[0:CHUNK, 5, 0:CHUNK], caus[0:CHUNK, 0:CHUNK],
                                            pb[b][0:CHUNK, P:P + CHUNK]).then_inc(read[b], 1)
                elif kind == "update":
                    if s != 3:
                        continue
                    h = a
                    for r in range(4):
                        wait_full(dve, g, last, ("update", h, r), banks(("update", h, r))[0])
                    if h:
                        wait_full(dve, g, last, ("read_out", h - 1, 1), 6)
                    dve.wait_ge(first_out, START + 16 * (B_HEADS * g + h))
                    dve.wait_ge(last_out, START + 16 * (B_HEADS * g + h))
                    link(dve.tensor_copy(st[:, 0, :], carry_s[:, h, :]))
                    for c in range(NCH):
                        r = [c in u for u in UPDATES].index(True)
                        i = UPDATES[r].index(c)
                        dst = carry_s[:, h, :] if c == NCH - 1 else s_first[:] if c == 0 else st[:, c + 1, :]
                        ins = dve.scalar_tensor_tensor(
                            out=dst, in0=st[:, c, :], scalar=decay[:, h, c:c + 1],
                            in1=pb[banks(("update", h, r))[0]][:, i * P:(i + 1) * P],
                            op0=ALU.mult, op1=ALU.add)
                        if c == 0:
                            ins.then_inc(first_made, 1)
                            dve.wait_ge(first_made, B_HEADS * g + h + 1)
                            dve.wait_ge(flags_in, 32 * (g + 1))
                            link(dve.memset(st[:, 1, :], 0.0))
                            link(dve.copy_predicated(st[:, 1, :], keep[:].broadcast_to([P, P]), s_first[:]))
                        elif c == NCH - 1:
                            ins.then_inc(last_made, 1)
                            dve.wait_ge(last_made, START + B_HEADS * g + h + 1)
                        elif c == 9:
                            ins.then_inc(read[7], 1)
                            wait_read(dve, g, last, ("update", h, 3), 7)
                        elif c == 6:
                            ins.then_inc(read[3], 1)
                            wait_read(dve, g, last, ("update", h, 0), 3)
                        elif c == 7:
                            ins.then_inc(read[4], 1)
                            wait_read(dve, g, last, ("update", h, 1), 4)
                        else:
                            link(ins)
                    dve.sem_inc(read[5], 1)
                elif kind == "finish":
                    h = a
                    wait_read(dve, g, last, ("sum_sq", h, 0), 3)
                    wait_read(dve, g, last, ("sum_sq", h, 1), 4)
                    dve.wait_ge(ob_copied, 2 * (B_HEADS * g + h + 1))
                    for r in range(2):
                        b = ("proj", f"bg{h}", r)
                        wait_read(dve, g, last, b, bank_of(last, b))
                    link(dve.reciprocal(rs[:], rs[:]))
                    link(dve.scalar_tensor_tensor(out=ob[:], in0=ob[:], scalar=gain_b[:, h:h + 1], in1=rs[:],
                                                  op0=ALU.mult, op1=ALU.mult))
                    link(dve.tensor_tensor(ob[:], ob[:], gate_b[:, h, :], ALU.mult))
                    split(gb_hi[:, h, :], gb_lo[:, h, :], ob[:]).then_inc(finished, 1)
                elif kind == "ya":
                    bank = bank_of(last, step)
                    lo, hi = sub(s)
                    wait_full(dve, g, last, step, bank)
                    wait_read(dve, g, last, ("ma", a, s), bank_of(last, ("ma", a, s)))
                    dve.tensor_tensor(sig_a[:, lo:hi], sig_a[:, lo:hi], pb[bank][:, 0:hi - lo],
                                      ALU.mult).then_inc(read[bank], 1)
                elif kind == "yb":
                    bank = bank_of(last, step)
                    lo, hi = sub(s)
                    wait_full(dve, g, last, step, bank)
                    wait_read(dve, g, last, ("mb", a, s), bank_of(last, ("mb", a, s)))
                    dve.tensor_tensor(sig_b[:, lo:hi], sig_b[:, lo:hi], pb[bank][:, 0:hi - lo],
                                      ALU.mult).then_inc(read[bank], 1)
                    wait_read(dve, g, last, step, bank)
                    wait_read(dve, g, last, ("ya", a, s), bank_of(last, ("ya", a, s)))
                    link(dve.tensor_tensor(sig_a[:, lo:hi], sig_a[:, lo:hi], sig_b[:, lo:hi], ALU.add))
                    if a == 0 and s == 0:
                        dve.wait_ge(finished, START + B_HEADS * (g + 1))
                    split(m_hi[:, a, lo:hi], m_lo[:, a, lo:hi], sig_a[:, lo:hi]).then_inc(merged, 1)
                elif kind == "out" and s == 3:
                    for i, (t0, n) in enumerate(TILES):
                        b = OUT_BANKS[i]
                        r = res[0:n, i, 512 * a:512 * a + 512]
                        wait_full(dve, g, last, ("out", a, 0), b)
                        dve.wait_ge(res_in[i], 16 * (g + 1))
                        dve.tensor_tensor(r, r, pb[b][0:n, :], ALU.add).then_inc(read[b], 1)
                        if a == 1:
                            wait_read(dve, g, last, ("out", 1, 0), b)
                            dve.sem_inc(summed, 1)
                            if i:
                                final_norm(g, i - 1)
                elif kind.startswith("x_"):
                    prepare_x(step, g, g + 1, last)
            final_norm(g, NT - 1)

        groups(dve, body)

    @block.tensor
    def _(pe):
        def three_pass(out, w_h, w_l, m_h, m_l, first, last_of_bank):
            pe.matmul(out, w_h, m_h, start=first, stop=False)
            pe.matmul(out, w_h, m_l, start=False, stop=False)
            return pe.matmul(out, w_l, m_h, start=False, stop=last_of_bank)

        def prepare_x(step, g, gn, last):
            kind, s, _ = step
            if kind == "x_sum":
                lo, hi = sub(s)
                b = 6 + s
                pe.wait_ge(x_summed, 2 * gn + s + 1)
                wait_bank_free(pe, g, last, step, b)
                pe.matmul(pb[b][:, 0:hi - lo], ones[:], x_acc[:, s, 0, 0:hi - lo],
                          start=True, stop=True).then_inc(full[b], 1)

        pe.wait_ge(consts_made, 1)
        for step in X_STEPS:
            prepare_x(step, None, 0, False)
        pe.wait_ge(consts_in, 16 * 9)

        def body(g, last):
            for step in steps(last):
                kind, a, s = step
                if kind == "proj" or kind in ("ma", "mb"):
                    b = BLOCK[a if kind == "proj" else f"{kind}{a}"]
                    bank = bank_of(last, step)
                    lo, hi = sub(s)
                    if a == "ak":
                        pe.wait_ge(x_split, 2 * g + s + 1)
                    if s == 0:
                        pe.wait_ge(w_split, NB * g + b + 1)
                    wait_bank_free(pe, g, last, step, bank)
                    for k in range(KT):
                        ins = three_pass(pb[bank][:, 0:hi - lo], w_hi[SLOT[b]][:, k, :], w_lo[SLOT[b]][:, k, :],
                                         x_hi[:, k, lo:hi], x_lo[:, k, lo:hi], k == 0, k == KT - 1)
                    ins.then_inc(full[bank], 1)
                elif kind in ("ya", "yb"):
                    b = BLOCK[f"wab{a}"]
                    bank = bank_of(last, step)
                    lo, hi = sub(s)
                    c0, c1 = SUBS[s]
                    if s == 0:
                        pe.wait_ge(w_split, NB * g + b + 1)
                        if kind == "ya":
                            pe.wait_ge(gated_a, START + 2 * A_GROUP * (g + 1))
                        else:
                            pe.wait_ge(finished, START + B_HEADS * (g + 1))
                    wait_bank_free(pe, g, last, step, bank)
                    for k in range(4):
                        if kind == "ya":
                            out = pb[bank][:, 0:hi - lo].rearrange("p (c t) -> p c t", t=CHUNK)
                            m_h, m_l = ga_hi[:, c0:c1, k, :], ga_lo[:, c0:c1, k, :]
                        else:
                            out = pb[bank][:, 0:hi - lo]
                            m_h, m_l = gb_hi[:, k, lo:hi], gb_lo[:, k, lo:hi]
                        kk = k + 4 * (kind == "yb")
                        ins = three_pass(out, w_hi[SLOT[b]][:, kk, :], w_lo[SLOT[b]][:, kk, :],
                                         m_h, m_l, k == 0, k == 3)
                    ins.then_inc(full[bank], 1)
                elif kind == "v_win":
                    cs = range(4 * a, min(4 * a + 4, NCH))
                    if a == 0:
                        pe.wait_ge(carried, g + 1)
                        for r in range(2):
                            b = ("proj", "av", r)
                            wait_read(pe, g, last, b, bank_of(last, b))
                    bank = banks(step)[0]
                    wait_bank_free(pe, g, last, step, bank)
                    for i, c in enumerate(cs):
                        ins = pe.transpose(pb[bank][:, i * P:(i + 1) * P], v_t[:, c * CHUNK:c * CHUNK + P], ident[:])
                    ins.then_inc(full[bank], 1)
                elif kind == "k_win":
                    pe.wait_ge(k_roped, g + 1)
                    wait_bank_free(pe, g, last, step, 4)
                    for i, c in enumerate((0, NCH - 1)):
                        ins = pe.transpose(pb[4][:, i * P:(i + 1) * P], k_rot[:, c * CHUNK:c * CHUNK + P], ident[:])
                    ins.then_inc(full[4], 1)
                elif kind == "scores":
                    c = a
                    if c == 0:
                        pe.wait_ge(q_roped, START + A_GROUP * (g + 1))
                    for v in range(A_KV):
                        wait_bank_free(pe, g, last, step, 3 + v)
                        rows = slice(HEAD_DIM * v, HEAD_DIM * (v + 1))
                        for i in range(2):
                            ins = pe.matmul(pb[3 + v][:, i * P:(i + 1) * P],
                                            q_rot[rows, c, 2 * i:2 * i + 2, :],
                                            k_rot[rows, c * CHUNK:c * CHUNK + P], start=True, stop=True)
                        ins.then_inc(full[3 + v], 1)
                elif kind == "probs_t":
                    pe.wait_ge(probs_norm, NCH * g + a + 1)
                    wait_bank_free(pe, g, last, step, 5)
                    for i in range(4):
                        ins = pe.transpose(pb[5][:, i * P:(i + 1) * P], probs[:, a % 2, i, :], ident[:])
                    ins.then_inc(full[5], 1)
                elif kind == "attend":
                    wait_read(pe, g, last, ("probs_t", a, 0), 5)
                    if a == 0:
                        wait_read(pe, g, last, ("v_win", 2, 0), 5)
                    wait_bank_free(pe, g, last, step, 6)
                    for v in range(A_KV):
                        rows = slice(HEAD_DIM * v, HEAD_DIM * (v + 1))
                        ins = pe.matmul(pb[6][rows, 0:2 * P], v_win[:, a, rows], probs_t[:, 2 * v:2 * v + 2, :],
                                        start=True, stop=True)
                    ins.then_inc(full[6], 1)
                elif kind in ("kend_t", "v_t"):
                    b = banks(step)[0]
                    src = rev if kind == "kend_t" else vb
                    if s == 0:
                        if kind == "kend_t":
                            pe.wait_ge(keys_made, B_HEADS * g + a + 1)
                        else:
                            for r in range(2):
                                n = ("proj", f"bi{a}", r)
                                wait_read(pe, g, last, n, bank_of(last, n))
                    wait_bank_free(pe, g, last, step, b)
                    for k, i in enumerate(range(4) if s == 0 else (4, 5)):
                        t0, n = TILES[i]
                        ins = pe.transpose(pb[b][0:n, k * P:(k + 1) * P], src[:, t0:t0 + n], ident[:])
                    ins.then_inc(full[b], 1)
                elif kind == "scores_b":
                    b = banks(step)[0]
                    if s == 0:
                        for r in range(2):
                            n = ("proj", f"bq{a}", r)
                            wait_read(pe, g, last, n, bank_of(last, n))
                    wait_bank_free(pe, g, last, step, b)
                    for k, i in enumerate(range(4) if s == 0 else (4, 5)):
                        t0, n = TILES[i]
                        ins = pe.matmul(pb[b][0:n, k * P:k * P + n], inv[:, t0:t0 + n], q_dec[:, a, t0:t0 + n],
                                        start=True, stop=True)
                    ins.then_inc(full[b], 1)
                elif kind == "update":
                    b = banks(step)[0]
                    if s == 0:
                        wait_read(pe, g, last, ("v_t", a, 0), 7)
                        wait_read(pe, g, last, ("v_t", a, 1), 6)
                    wait_bank_free(pe, g, last, step, b)
                    for i, c in enumerate(UPDATES[s]):
                        rows = slice(CHUNK * (c % 2), CHUNK * (c % 2 + 1))
                        ins = pe.matmul(pb[b][:, i * P:(i + 1) * P], kend_tok[rows, c // 2, :],
                                        v_tok[rows, c // 2, :], start=True, stop=True)
                    ins.then_inc(full[b], 1)
                elif kind == "read_out":
                    b = banks(step)[0]
                    if s == 0:
                        pe.wait_ge(last_made, START + B_HEADS * g + a + 1)
                        wait_read(pe, g, last, ("scores_b", a, 0), 3)
                        wait_read(pe, g, last, ("scores_b", a, 1), 4)
                    wait_bank_free(pe, g, last, step, b)
                    tiles = range(4) if s == 0 else (4, 5)
                    for k, i in enumerate(tiles):
                        n = TILES[i][1]
                        pe.matmul(pb[b][:, k * P:k * P + n], v_tok[0:n, i, :], sc_t[0:n, i, 0:n],
                                  start=(k == 0), stop=False, skip_group_check=True)
                    chunks = range(8) if s == 0 else range(8, NCH)
                    for k, c in enumerate(chunks):
                        ins = pe.matmul(pb[b][:, k * CHUNK:(k + 1) * CHUNK], st[:, c, :],
                                        q_dec[:, a, c * CHUNK:(c + 1) * CHUNK],
                                        start=False, stop=(c == chunks[-1]), skip_group_check=True)
                    ins.then_inc(full[b], 1)
                elif kind == "sum_sq":
                    b = banks(step)[0]
                    lo, hi = (0, 512) if s == 0 else (512, T)
                    wait_read(pe, g, last, ("read_out", a, s), 7 - s)
                    wait_bank_free(pe, g, last, step, b)
                    pe.matmul(pb[b][:, 0:hi - lo], ones[:], sq[:, lo:hi], start=True, stop=True).then_inc(full[b], 1)
                elif kind == "out":
                    b = BLOCK[f"wo{a}{s}"]
                    pe.wait_ge(w_split, NB * g + b + 1)
                    if a == 0:
                        pe.wait_ge(merged, START + 2 * MERGES * g + 4 * (s + 1))
                    wh = w_hi[SLOT[b]][:].rearrange("p k c -> p (k c)")
                    wl = w_lo[SLOT[b]][:].rearrange("p k c -> p (k c)")
                    for i, (t0, n) in enumerate(TILES):
                        bank = OUT_BANKS[i]
                        if s == 0:
                            wait_bank_free(pe, g, last, step, bank)
                        for k in range(2):
                            kt = 2 * s + k
                            mh, ml = m_hi[:, kt, t0:t0 + n], m_lo[:, kt, t0:t0 + n]
                            cols = slice(512 * k, 512 * k + 512)
                            pe.matmul(pb[bank][0:n, :], mh, wh[:, cols], start=(kt == 0), stop=False)
                            pe.matmul(pb[bank][0:n, :], mh, wl[:, cols], start=False, stop=False)
                            ins = pe.matmul(pb[bank][0:n, :], ml, wh[:, cols], start=False, stop=(kt == KT - 1))
                        if s == 3:
                            ins.then_inc(full[bank], 1)
                    pe.drain().then_inc(piece_used, 1)
                elif kind.startswith("x_"):
                    prepare_x(step, g, g + 1, last)

        groups(pe, body)

    ctx.close()


def rope_tables():
    import numpy as np
    half = ROPE_DIM // 2
    inv = np.power(np.float32(ROPE_THETA), -np.arange(half, dtype=np.float32) * np.float32(2.0 / ROPE_DIM))
    pos = np.concatenate([PAST_LEN + np.arange(DEC_SEQ), np.arange(SEQ)]).astype(np.float32)
    ang = (inv.astype(np.float32)[:, None] * pos[None, :]).astype(np.float32).astype(np.float64)
    cos = np.ones((HEAD_DIM, pos.size), np.float32)
    sin = np.zeros((HEAD_DIM, pos.size), np.float32)
    cos[:half], cos[half:ROPE_DIM] = np.cos(ang), np.cos(ang)
    sin[:half], sin[half:ROPE_DIM] = -np.sin(ang), np.sin(ang)
    return [np.ascontiguousarray(np.tile(t, (A_KV, 1)).reshape(P, GROUPS, T).transpose(1, 0, 2))
            for t in (cos, sin)]


def layouts(i):
    import numpy as np
    w_in, w_ba, w_bb, w_out = i["w_in"][0], i["w_branch_a"][0], i["w_branch_b"][0], i["w_out"][0]

    def heads(rows):
        return rows.reshape(A_KV, A_GROUP, HEAD_DIM, -1).transpose(1, 0, 2, 3).reshape(A_GROUP, P, -1)

    def tiled(cols):
        return cols.reshape(KT, P, P).transpose(1, 0, 2)

    cut = np.split(w_in, np.cumsum([512, 128, 128, 512, 512, 512, 512, 512, D_MODEL]), axis=1)
    names = ["aq", "ak", "av", "ag", "bq", "bf", "bi", "bg", "ma", "mb"]
    cut = dict(zip(names, cut))
    by_head = {n: heads(np.ascontiguousarray(cut[n].T)) for n in ("aq", "ag")}
    w_a = heads(w_ba)
    w_b = w_bb.reshape(B_HEADS, P, D_MODEL)
    blocks = []
    for n in BLOCKS:
        if n in ("ak", "av"):
            blocks.append(tiled(cut[n]))
        elif n[:2] in ("aq", "ag"):
            blocks.append(tiled(by_head[n[:2]][int(n[2:])].T))
        elif n.startswith("wab"):
            c = slice(P * int(n[3:]), P * (int(n[3:]) + 1))
            blocks.append(np.concatenate([w_a[:, :, c], w_b[:, :, c]]).transpose(1, 0, 2))
        elif n.startswith("wo"):
            hf, kp = int(n[2]), int(n[3])
            rows = w_out[2 * P * kp:2 * P * (kp + 1), 512 * hf:512 * (hf + 1)]
            blocks.append(rows.reshape(2, P, 512).transpose(1, 0, 2).reshape(P, KT, P))
        else:
            c = slice(P * int(n[2:]), P * (int(n[2:]) + 1))
            blocks.append(tiled(cut[n[:2]][:, c]))
    x = np.concatenate([i["x_sample"][0], i["x_prompt"][0]]).reshape(GROUPS, T, D_MODEL)
    old = WINDOW - CHUNK
    cache_k = i["cache_attn_k"][0, 0, old:].reshape(CHUNK, P).T
    cache_v = i["cache_attn_v"][0, 0, old:].reshape(CHUNK, P).T
    j = np.arange(P)[:, None] // CHUNK
    col = np.arange(4)[None, :]
    sinks = i["attn_sinks"][0][(col // 2) * A_GROUP + 2 * (col % 2) + j]
    cos, sin = rope_tables()
    tok = np.arange(P)
    causal = ((tok[:, None] <= tok[None, :]) & (tok[:, None] // CHUNK == tok[None, :] // CHUNK))
    first = np.zeros((GROUPS, P, 1), np.float32)
    first[0] = NEG_INF
    keep = np.ones((GROUPS, P, 1), np.int32)
    keep[0] = 0
    return {
        "x": x, "x_t": x.reshape(GROUPS, T, KT, P).transpose(0, 3, 2, 1), "w": np.stack(blocks), "cache_k": cache_k, "cache_v": cache_v,
        "state": i["state_hgrn"][0, 0].transpose(1, 0, 2),
        "norm_gain": i["norm_gain"][0].reshape(KT, P).T, "sinks": sinks,
        "lb_logits": i["hgrn_lb_logits"].reshape(2, B_HEADS, P).transpose(2, 0, 1),
        "hgrn_gain": i["hgrn_norm_gain"][0].reshape(B_HEADS, P).T,
        "final_gain": np.broadcast_to(i["final_norm_gain"], (P, D_MODEL)),
        "rope_cos": cos, "rope_sin": sin, "causal": causal.astype(np.int32),
        "identity": np.eye(P, dtype=np.float32), "first_mask": first, "keep_state": keep,
    }


OUTPUTS = {
    "y": (GROUPS, T, D_MODEL), "win_k": (GROUPS, 2, P, P), "win_v": (GROUPS, 2, P, P),
    "state_first": (GROUPS, B_HEADS, P, P), "state_last": (GROUPS, B_HEADS, P, P),
}


def kernel(**inputs):
    import numpy as np
    from concourse import bacc
    from concourse.bass_utils import run_bass_kernel_spmd

    arrays = {n: np.ascontiguousarray(a) for n, a in layouts({k: np.asarray(v) for k, v in inputs.items()}).items()}
    nc = bacc.Bacc("TRN2", target_bir_lowering=False, num_devices=1)
    args = {n: nc.dram_tensor(f"in_{n}", a.shape, mybir.dt.from_np(a.dtype), kind="ExternalInput").ap()
            for n, a in arrays.items()}
    outs = {n: nc.dram_tensor(f"out_{n}", shape, F32, kind="ExternalOutput").ap() for n, shape in OUTPUTS.items()}
    program(nc, **args, **outs)
    r = run_bass_kernel_spmd(nc, [{f"in_{n}": a for n, a in arrays.items()}], core_ids=[0]).results[0]
    got = {n: r[f"out_{n}"] for n in OUTPUTS}
    y = got["y"].reshape(DEC_SEQ + SEQ, D_MODEL)
    window = (1, 1, WINDOW, A_KV, HEAD_DIM)
    return (y[DEC_SEQ:].reshape(1, SEQ, D_MODEL), y[:DEC_SEQ].reshape(1, DEC_SEQ, D_MODEL),
            got["win_k"][-1, 1].reshape(window), got["win_v"][-1, 1].reshape(window),
            got["state_last"][-1][None, None],
            got["win_k"][0, 0].reshape(window), got["win_v"][0, 0].reshape(window),
            got["state_first"][0][None, None])
```

```python
from contextlib import ExitStack

import concourse.mybir as mybir

F32 = mybir.dt.float32
F32R = mybir.dt.float32r
BF16 = mybir.dt.bfloat16
I32 = mybir.dt.int32
ACT = mybir.ActivationFunctionType
ALU = mybir.AluOpType
AX = mybir.AxisListType

P = 128
D_MODEL = 1024
SEQ, DEC_SEQ = 2048, 64
CHUNK = 64
EPS = 1e-6
NEG_INF = -1e30
WINDOW = 128
HEAD_DIM = 64
A_KV = 2
A_GROUP = 4
ATTN_SCALE = HEAD_DIM ** -0.5
ROPE_DIM = HEAD_DIM // 4
ROPE_THETA = 500000.0
PAST_LEN = 512
B_HEADS = 4

CHUNKS = (SEQ + DEC_SEQ) // CHUNK
GROUPS = 3
NCH = CHUNKS // GROUPS
T = NCH * CHUNK
SUBS = [(0, 5), (5, NCH)]
HALF = max(b - a for a, b in SUBS) * CHUNK
KT = D_MODEL // P
TILES = [(i * P, min(P, T - i * P)) for i in range((T + P - 1) // P)]
NT = len(TILES)
MERGES = D_MODEL // P
START = 16

BLOCKS = (["ak", "av", "bf0"] + [f"aq{j}" for j in range(A_GROUP)]
          + [f"{n}{h}" for h in range(B_HEADS) for n in ("bf", "bq", "bi", "bg")][1:]
          + [f"ag{j}" for j in range(A_GROUP)]
          + [f"{n}{j}" for j in range(MERGES) for n in ("ma", "mb", "wab")]
          + [f"wo{hf}{kp}" for hf in range(2) for kp in range(KT // 2)])
NB = len(BLOCKS)
BLOCK = {n: b for b, n in enumerate(BLOCKS)}
SLOTS = 4
SKIP = [BLOCK[f"mb{j}"] for j in range(-(-NB // SLOTS) * SLOTS - NB)]
SLOT = [(b + sum(b >= k for k in SKIP)) % SLOTS for b in range(NB)]


def before(b):
    older = [c for c in range(b) if SLOT[c] == SLOT[b]]
    return (older[-1], 0) if older else (max(c for c in range(NB) if SLOT[c] == SLOT[b]), 1)


def nth_in_slot(b):
    return sum(SLOT[c] == SLOT[b] for c in range(b))


FIRST = 3
PER_SLOT = [sum(s == k for s in SLOT) for k in range(SLOTS)]

X_STEPS = [("x_square", 0, 0), ("x_sum", 0, 0), ("x_square", 1, 0), ("x_split", 0, 0),
           ("x_sum", 1, 0), ("x_split", 1, 0)]
OUT_BANKS = [3, 4, 5, 0, 1, 2]


def steps(last):
    out = []

    def block(n):
        return [(kind, n, s) for s in range(2) for kind in ("proj", "evac")]

    hgrn = [["kend_t0", "kend_t1"], ["v_t0", "v_t1"], ["scores_b0", "scores_b1"], ["update0"],
            [], ["read_out0", "read_out1"], [], ["sum_sq0", "sum_sq1"]]

    def recurrence(n, h):
        return [(k[:-1], h, int(k[-1])) for k in hgrn[n]] if h >= 0 else []

    out += [(kind, n, s) for s in range(2) for n in ("ak", "av", "bf0") for kind in ("proj", "evac")]
    for n in ["aq0", "aq1"]:
        out += block(n)
    out += [("v_win", r, 0) for r in range(3)] + [("k_win", 0, 0)]
    for n in ["aq2", "aq3"]:
        out += block(n)
    heads = [(f"{n}{h}", s) for h in range(B_HEADS) for n in ("bf", "bq", "bi", "bg") for s in range(2)]
    for n, half in list(enumerate(heads))[2:]:
        h, i, k = n // 8, n % 8, (n - 2) // 2
        out.append(("proj", *half))
        chunk = [("attend", k - 2, 0)] if n % 2 else [("probs_t", k - 2, 0), ("scores", k, 0)]
        parts = [[t for t in chunk if 0 <= t[1] < NCH], [("evac", *half)], recurrence(i, h - 1)]
        order = {0: (2, 0, 1), 3: (0, 1, 2)}.get(i, (0, 2, 1))
        out += [t for j in order for t in parts[j]]
        if n % 2 == 0:
            out += [(kind, c, 0) for kind, c in (("softmax", k), ("normalise", k - 1)) if 0 <= c < NCH]
        if i == 4:
            out.append(("keys", h, 0))
        if i == 0 and h >= 2:
            out.append(("finish", h - 2, 0))
    gates = [(f"ag{j}", s) for j in range(A_GROUP) for s in range(2)]
    for n, half in enumerate(gates):
        parts = [("evac", *half)], recurrence(n, B_HEADS - 1)
        out += [("proj", *half)] + (parts[1] + parts[0] if n == 1 else parts[0] + parts[1])
        if n == 4:
            out.append(("finish", B_HEADS - 2, 0))
    out.append(("finish", B_HEADS - 1, 0))
    for j in range(MERGES):
        out += [(n, j, s) for n in ("ma", "mb", "ya", "yb") for s in range(2)]
    for p in range(KT):
        if not last:
            out += {0: X_STEPS[:1], 1: X_STEPS[1:2], 2: X_STEPS[2:4], 4: X_STEPS[4:]}.get(p, [])
        out.append(("out", p // 4, p % 4))
    return out


def banks(step):
    kind, a, b = step
    return {"v_win": [7 - a], "k_win": [4], "scores": [3, 4], "probs_t": [5], "attend": [6],
            "kend_t": [7 - b], "v_t": [7 - b], "scores_b": [7 - 2 * b], "update": [3, 4, 5, 6, 7],
            "read_out": [7 - b], "sum_sq": [7 - 2 * b], "x_sum": [6 + a]}.get(kind, [])


def plan(last):
    count, use, proj = [0] * 8, {}, 0
    place = {}
    for s in steps(last):
        if s[0] in ("proj", "ma", "mb", "ya", "yb"):
            bs, proj = [proj % 3], proj + 1
        elif s[0] == "out":
            bs = OUT_BANKS if s[2] == 0 else []
        else:
            bs = banks(s) if s[0] != "evac" else []
        place[s] = bs
        for b in bs:
            use[s, b] = count[b]
            count[b] += 1
    return use, place, count


PLAN = {last: plan(last) for last in (False, True)}
USES = PLAN[False][2]
PRIOR = [int(b in (6, 7)) for b in range(8)]
UPDATE_BANKS = {5: [0, 2], 3: [4, 6], 4: [1, 3, 5, 7], 7: [8, 10], 6: [9]}
UPDATE_BANK = {c: b for b, cs in UPDATE_BANKS.items() for c in cs}


def program(nc, x, x_t, w, cache_k, cache_v, state, norm_gain, sinks, lb_logits, hgrn_gain, final_gain,
            rope_cos, rope_sin, causal, identity, first_mask, keep_state,
            y, win_k, win_v, state_first, state_last):
    ctx = ExitStack()
    base = (nc.sbuf_base + 31) // 32 * 32
    top = [base]

    def sb(name, shape, dt=F32, at=None):
        size = 2 if dt == BF16 else 4
        for n in shape[1:]:
            size *= n
        size = (size + 31) // 32 * 32
        if at is None:
            at = top[0]
            top[0] += size
        return nc.alloc_sbuf_tensor_at(name, shape, dt, offset=at), at, at + size

    def own(name, shape, dt=F32, at=None):
        return sb(name, shape, dt, at)[0]

    x_hi = own("x_hi", [P, KT, T], F32R)
    x_lo, at_x_lo, _ = sb("x_lo", [P, KT, T], F32R)
    x_raw = own("x_raw", [P, KT, T], F32, at_x_lo)
    ga_hi, at_ga_hi, _ = sb("ga_hi", [P, NCH, A_GROUP, CHUNK], F32R)
    gb_hi, at_gb_hi, _ = sb("gb_hi", [P, B_HEADS, T], F32R)
    ga_lo, at_ga_lo, _ = sb("ga_lo", [P, NCH, A_GROUP, CHUNK], F32R)
    gb_lo, at_gb_lo, _ = sb("gb_lo", [P, B_HEADS, T], F32R)
    q_rot = own("q_rot", [P, NCH, A_GROUP, CHUNK], F32, at_ga_hi)
    attn_o = own("attn_o", [P, NCH, A_GROUP, CHUNK], F32, at_ga_lo)
    q_dec = own("q_dec", [P, B_HEADS, T], F32, at_gb_hi)
    gate_b = own("gate_b", [P, B_HEADS, T], F32, at_gb_lo)
    res = own("res", [P, NT, D_MODEL], F32, at_ga_hi)
    w_hi, w_lo, w_raw = [], [], []
    for s in range(SLOTS):
        w_hi.append(own(f"w_hi{s}", [P, KT, P], F32R))
        t, at, _ = sb(f"w_lo{s}", [P, KT, P], F32R)
        w_lo.append(t)
        w_raw.append(own(f"w_raw{s}", [P, KT, P], F32, at))
    fgain = own("fgain", [P, D_MODEL])
    ident, ones = own("ident", [P, P]), own("ones", [P, P])
    ones_r = own("ones_r", [P, P], F32R)
    caus = own("caus", [P, P], I32)
    start_f = own("start_f", [P, T])
    end_one = own("end_one", [P, T], BF16)
    carry_s = own("carry_s", [P, B_HEADS, P])
    carry_k, carry_v = own("carry_k", [P, CHUNK]), own("carry_v", [P, CHUNK])
    s_first = own("s_first", [P, P])
    decay = own("decay", [P, B_HEADS, NCH])
    gain, gain_b = own("gain", [P, KT]), own("gain_b", [P, B_HEADS])
    sink, neg_sink = own("sink", [P, 4]), own("neg_sink", [P, 4])
    lb, one_lb, logit = own("lb", [P, 4]), own("one_lb", [P, 4]), own("logit", [P, 2, 4])
    eps, pad, root = own("eps", [P, 1]), own("pad", [P, 1]), own("root", [P, 1])
    amask, keep = own("amask", [P, 1]), own("keep", [P, 1], I32)
    rmax, nmax, sarg = own("rmax", [P, 2, 4]), own("nmax", [P, 2, 4]), own("sarg", [P, 2, 4])
    psum_, esink, rden = own("psum_", [P, 2, 4]), own("esink", [P, 2, 4]), own("rden", [P, 2, 4])
    yss = own("yss", [P, NT])
    region = top[0]
    f, _, _ = sb("f", [P, T + 1])
    prod, rev, inv = own("prod", [P, T]), own("rev", [P, T]), own("inv", [P, T])
    keyb = own("keyb", [P, T])
    vb = own("vb", [P, T])
    kend_tok, v_tok, sc_t = own("kend_tok", [P, NT, P]), own("v_tok", [P, NT, P]), own("sc_t", [P, NT, P])
    st = own("st", [P, NCH, P])
    sq, at_sq, _ = sb("sq", [P, T])
    sq_lo = own("sq_lo", [P, T], F32R, at_sq)
    sq_hi, rs, ob = own("sq_hi", [P, T], F32R), own("rs", [P, T]), own("ob", [P, T])
    merged_bytes = 2 * MERGES * T * 4
    assert top[0] - region <= merged_bytes, (top[0] - region, merged_bytes)
    top[0] = region + merged_bytes
    m_hi = own("m_hi", [P, MERGES, T], F32R, region)
    m_lo = own("m_lo", [P, MERGES, T], F32R, region + merged_bytes // 2)
    attn_at = top[0]
    k_rot, v_t = own("k_rot", [P, T + CHUNK]), own("v_t", [P, T + CHUNK])
    v_win = own("v_win", [P, NCH, P])
    probs = own("probs", [P, 2, 4, P])
    probs_t = own("probs_t", [P, 4, P])
    k_win = own("k_win", [P, 2, P])
    swap, raw = own("swap", [P, T]), own("raw", [P, T])
    attn_end = top[0]
    top[0] = attn_at
    sig_a, sig_b = own("sig_a", [P, T]), own("sig_b", [P, T])
    scratch = own("scratch", [P, D_MODEL])
    x_acc = own("x_acc", [P, 2, 2, HALF])
    x_sq = own("x_sq", [P, 2, 2, HALF])
    assert top[0] <= attn_end, (top[0], attn_end)
    top[0] = attn_end
    cos, sin = own("cos", [P, T]), own("sin", [P, T])
    assert top[0] <= nc.sbuf_usable_end, (top[0], nc.sbuf_usable_end)

    pb = [nc.alloc_psum_tensor(f"bank{b}", [P, 512], F32) for b in range(8)]

    full = [nc.alloc_semaphore(f"bank{b}_full") for b in range(8)]
    read = [nc.alloc_semaphore(f"bank{b}_read") for b in range(8)]
    sem = nc.alloc_semaphore
    w_landed = [sem(f"w_landed{s}") for s in range(SLOTS)]
    w_high, w_split = sem("w_high"), sem("w_split")
    piece_used = sem("piece_used")
    consts_in, consts_made = sem("consts_in"), sem("consts_made")
    lb_max, lb_exp, lb_made = sem("lb_max"), sem("lb_exp"), sem("lb_made")
    rope_in, flags_in = sem("rope_in"), sem("flags_in")
    k_roped, q_roped, raw_free = sem("k_roped"), sem("q_roped"), sem("raw_free")
    windows_out = sem("windows_out")
    carried = sem("carried")
    row_max, probs_exp, probs_norm = sem("row_max"), sem("probs_exp"), sem("probs_norm")
    f_used, keys_made = sem("f_used"), sem("keys_made")
    sig_made = sem("sig_made")
    sq_high, sq_split = sem("sq_high"), sem("sq_split")
    first_made, first_out, last_made, last_out = (sem("first_made"), sem("first_out"),
                                                  sem("last_made"), sem("last_out"))
    ob_copied, finished, gated_a = sem("ob_copied"), sem("finished"), sem("gated_a")
    merged = sem("merged")
    x_landed = [[sem(f"x_landed{s}{q}") for q in range(4)] for s in range(2)]
    x_squared, x_added, x_summed = [[sem(f"{n}{s}") for s in range(2)]
                                    for n in ("x_squared", "x_added", "x_summed")]
    x_scaled, x_high, x_split = sem("x_scaled"), sem("x_high"), sem("x_split")
    gain_in, logit_in = sem("gain_in"), sem("logit_in")
    res_in = [sem(f"res_in{i}") for i in range(NT)]
    summed, y_root, y_made, y_out = sem("summed"), sem("y_root"), sem("y_made"), sem("y_out")
    act_step, dve_step = sem("act_step"), sem("dve_step")

    def use(g, last, step, b):
        if g is None:
            return 0
        return PRIOR[b] + USES[b] * g + PLAN[last][0][step, b]

    def wait_full(eng, g, last, step, b):
        eng.wait_ge(full[b], use(g, last, step, b) + 1)

    def wait_read(eng, g, last, step, b):
        eng.wait_ge(read[b], START + use(g, last, step, b) + 1)

    def wait_block_read(eng, g, last, name):
        halves = [("proj", name, s) for s in range(2)]
        if bank_of(last, halves[0]) != bank_of(last, halves[1]):
            wait_read(eng, g, last, halves[0], bank_of(last, halves[0]))
        wait_read(eng, g, last, halves[1], bank_of(last, halves[1]))

    def wait_bank_free(eng, g, last, step, b):
        eng.wait_ge(read[b], START + use(g, last, step, b))

    def bank_of(last, step):
        return PLAN[last][1][step][0]

    def sub(s):
        return SUBS[s][0] * CHUNK, SUBS[s][1] * CHUNK

    def last_step_of(b):
        n = BLOCKS[b]
        if n.startswith("wab"):
            return ("yb", int(n[3:]), 1)
        if n[:2] in ("ma", "mb"):
            return (n[:2], int(n[2:]), 1)
        return ("proj", n, 1)

    def groups(eng, body):
        with eng.Fori(0, GROUPS - 1) as g:
            body(g, False)
        body(GROUPS - 1, True)

    def add_squares(eng, s, gn):
        n = sub(s)[1] - sub(s)[0]
        v = x_acc[:, s, :, 0:n]
        for q in range(1, 4):
            eng.wait_ge(x_squared[s], 4 * gn + q + 1)
            eng.tensor_tensor(v, v, x_sq[:, (3 * s + q - 1) % 2, :, 0:n], ALU.add).then_inc(x_added[s], 1)
            eng.wait_ge(x_added[s], 3 * gn + q)
        eng.tensor_tensor(v[:, 0], v[:, 0], v[:, 1], ALU.add).then_inc(x_summed[s], 1)

    block = ctx.enter_context(nc.Block())

    @block.sync
    def _(sp):
        def load_block(g, b, slots_wait, last=False):
            if slots_wait:
                c, back = before(b)
                gg = g - back
                if BLOCKS[c].startswith("wo"):
                    hf, kp = int(BLOCKS[c][2]), int(BLOCKS[c][3])
                    sp.wait_ge(piece_used, 8 * gg + 4 * hf + kp + 1)
                else:
                    s = last_step_of(c)
                    wait_full(sp, gg, last, s, bank_of(last, s))
            sp.dma_start(w_raw[SLOT[b]][:], w[b]).then_inc(w_landed[SLOT[b]], 16)

        def fetch_x(g, s):
            lo, hi = sub(s)
            for q in range(4):
                k = slice(2 * q, 2 * q + 2)
                sp.dma_start(x_raw[:, k, lo:hi], x_t[g, :, k, lo:hi]).then_inc(x_landed[s][q], 16)

        fetch_x(0, 0)
        sp.dma_start(gain[:], norm_gain).then_inc(gain_in, 16)
        load_block(0, 0, False)
        fetch_x(0, 1)
        load_block(0, 1, False)
        load_block(0, 2, False)
        for t, a in ((carry_k, cache_k), (carry_v, cache_v), (ident, identity), (caus, causal),
                     (gain_b, hgrn_gain), (sink, sinks), (carry_s, state),
                     (fgain, final_gain)):
            sp.dma_start(t[:], a).then_inc(consts_in, 16)
        load_block(0, 3, False)

        def body(g, last):
            sp.wait_ge(q_roped, START + A_GROUP * g)
            sp.dma_start(cos[:], rope_cos[g]).then_inc(rope_in, 16)
            sp.dma_start(sin[:], rope_sin[g]).then_inc(rope_in, 16)
            sp.wait_ge(row_max, START + NCH * g)
            sp.dma_start(amask[:], first_mask[g]).then_inc(flags_in, 16)
            sp.wait_ge(last_made, START + B_HEADS * g)
            sp.dma_start(keep[:], keep_state[g]).then_inc(flags_in, 16)
            for b in range(SLOTS, NB):
                load_block(g, b, True, last)
                if b == NB - 6 and not last:
                    s = ("mb", MERGES - 1, 1)
                    wait_full(sp, g, last, s, bank_of(last, s))
                    fetch_x(g + 1, 0)
                    fetch_x(g + 1, 1)
                if b == NB - 5:
                    s = ("yb", MERGES - 1, 1)
                    wait_full(sp, g, last, s, bank_of(last, s))
                    for i, (t0, n) in enumerate(TILES):
                        sp.dma_start(res[0:n, i, :], x[g, t0:t0 + n, :]).then_inc(res_in[i], 16)
            if not last:
                for b in range(SLOTS):
                    load_block(g + 1, b, True)
            for i, (t0, n) in enumerate(TILES):
                sp.wait_ge(y_made, NT * g + i + 1)
                sp.dma_start(y[g, t0:t0 + n, :], res[0:n, i, :]).then_inc(y_out, 16)

        groups(sp, body)
        sp.wait_ge(y_out, START + 16 * NT * GROUPS)
        sp.wait_ge(windows_out, 16 * 4 * GROUPS)
        sp.wait_ge(first_out, START + 16 * B_HEADS * GROUPS)
        sp.wait_ge(last_out, START + 16 * B_HEADS * GROUPS)

    @block.gpsimd
    def _(pool):
        for signal in (*read, raw_free, f_used, finished, merged, gated_a, first_out, last_out, y_out,
                       row_max, q_roped, last_made):
            pool.sem_inc(signal, START)

        def low(g, b):
            s = SLOT[b]
            pool.wait_ge(w_high, NB * g + b + 1)
            pool.tensor_tensor(w_lo[s][:], w_raw[s][:], w_hi[s][:].bitcast(F32), ALU.subtract).then_inc(w_split, 1)

        def body(g, last):
            for b in range(FIRST, NB):
                low(g, b)
                if b == NB - 5 and not last:
                    add_squares(pool, 1, g + 1)
            if not last:
                for b in range(FIRST):
                    low(g + 1, b)

        low(0, 0)
        add_squares(pool, 1, 0)
        for b in range(1, FIRST):
            low(0, b)
        groups(pool, body)

    @block.scalar
    def _(act):
        links = [0]

        def link(ins):
            links[0] += 1
            ins.then_inc(act_step, 1)
            act.wait_ge(act_step, links[0])

        def high(g, b):
            s = SLOT[b]
            act.wait_ge(w_landed[s], 16 * (PER_SLOT[s] * g + nth_in_slot(b) + 1))
            act.activation(w_hi[s][:], w_raw[s][:], ACT.Copy).then_inc(w_high, 1)

        def prepare_x(step, g, gn, last):
            kind, s, _ = step
            lo, hi = sub(s)
            n = hi - lo
            if kind == "x_square":
                for q in range(4):
                    act.wait_ge(x_landed[s][q], 16 * (gn + 1))
                    dst = x_acc[:, s, :, 0:n]
                    if q:
                        k = 3 * s + q - 1
                        dst = x_sq[:, k % 2, :, 0:n]
                        if k >= 2:
                            act.wait_ge(*((x_added[s], 3 * gn + q - 2) if q == 3 else (x_summed[0], gn + 1)))
                    act.activation(dst, x_raw[:, 2 * q:2 * q + 2, lo:hi], ACT.Square).then_inc(x_squared[s], 1)
            elif kind == "x_sum":
                b = 6 + s
                wait_full(act, g, last, step, b)
                act.activation(x_acc[:, s, 1, 0:n], pb[b][:, 0:n], ACT.Sqrt, scale=1.0 / D_MODEL,
                               bias=eps[:]).then_inc(read[b], 1)
            else:
                for q in range(4):
                    k = slice(2 * q, 2 * q + 2)
                    act.wait_ge(x_scaled, 8 * gn + 4 * s + q + 1)
                    act.activation(x_hi[:, k, lo:hi], x_raw[:, k, lo:hi], ACT.Copy).then_inc(x_high, 1)

        act.dma_start(logit[:], lb_logits).then_inc(logit_in, 16)
        act.wait_ge(lb_max, 1)
        act.activation(logit[:], logit[:], ACT.Exp).then_inc(lb_exp, 1)
        act.wait_ge(consts_made, 1)
        act.activation(root[:], eps[:], ACT.Sqrt)
        for step in X_STEPS:
            prepare_x(step, None, 0, False)
            if step == ("x_square", 0, 0):
                high(0, 0)
            if step == ("x_split", 0, 0):
                for b in range(1, FIRST):
                    high(0, b)

        def body(g, last):
            act.sem_clear(act_step)
            links[0] = 0

            def ahead(n):
                b = BLOCK[n] + 2
                if b < NB:
                    if b >= FIRST:
                        high(g, b)
                elif not last:
                    high(g + 1, b - NB)

            for step in steps(last):
                kind, a, s = step
                if kind == "evac":
                    step = ("proj", a, s)
                    if s == (a in ("av", "bf0")):
                        ahead(a)
                    bank = bank_of(last, step)
                    lo, hi = sub(s)
                    src = pb[bank][:, 0:hi - lo]
                    n = a[:2]
                    if n in ("ak", "aq"):
                        i = 0 if n == "ak" else 1 + int(a[2:])
                        wait_full(act, g, last, step, bank)
                        if s == 0:
                            act.wait_ge(raw_free, START + 5 * g + i)
                            if n == "ak":
                                act.wait_ge(gated_a, START + 2 * A_GROUP * g)
                        act.activation(raw[:, lo:hi], src, ACT.Copy).then_inc(read[bank], 1)
                    elif n == "av":
                        wait_full(act, g, last, step, bank)
                        act.activation(v_t[:, CHUNK + lo:CHUNK + hi], src, ACT.Copy).then_inc(read[bank], 1)
                    elif n == "bf":
                        h = int(a[2:])
                        wait_full(act, g, last, step, bank)
                        act.wait_ge(f_used, START + B_HEADS * g + h)
                        act.activation(f[:, lo:hi], src, ACT.Sigmoid).then_inc(read[bank], 1)
                    elif n == "bi":
                        wait_full(act, g, last, step, bank)
                        act.activation(vb[:, lo:hi], src, ACT.Copy).then_inc(read[bank], 1)
                    elif n == "bg":
                        h = int(a[2:])
                        wait_full(act, g, last, step, bank)
                        act.activation(gate_b[:, h, lo:hi], src, ACT.Sigmoid).then_inc(sig_made, 1)
                    elif n == "ag":
                        j = int(a[2:])
                        wait_full(act, g, last, step, bank)
                        if j:
                            act.wait_ge(gated_a, START + 2 * A_GROUP * g + 2 * j + s - 1)
                        else:
                            act.wait_ge(raw_free, START + 5 * (g + 1))
                        act.activation(raw[:, lo:hi], src, ACT.Sigmoid).then_inc(sig_made, 1)
                elif kind == "v_win":
                    cs = range(4 * a, min(4 * a + 4, NCH))
                    b = banks(step)[0]
                    wait_full(act, g, last, step, b)
                    act.activation(v_win[:, cs[0]:cs[-1] + 1, :], pb[b][:, 0:P * len(cs)].rearrange(
                        "p (c d) -> p c d", d=P), ACT.Copy).then_inc(read[b], 1)
                elif kind == "k_win":
                    wait_full(act, g, last, step, 4)
                    act.activation(k_win[:], pb[4][:, 0:2 * P].rearrange("p (c d) -> p c d", d=P),
                                   ACT.Copy).then_inc(read[4], 1)
                    wait_read(act, g, last, step, 4)
                    wait_read(act, g, last, ("v_win", 2, 0), 5)
                    for i, c in enumerate((0, NCH - 1)):
                        act.dma_start(win_k[g, i], k_win[:, i, :]).then_inc(windows_out, 16)
                        act.dma_start(win_v[g, i], v_win[:, c, :]).then_inc(windows_out, 16)
                elif kind == "softmax":
                    c = a
                    k = c % 2
                    act.wait_ge(row_max, START + NCH * g + c + 1)
                    if c >= 2:
                        wait_full(act, g, last, ("probs_t", c - 2, 0), 5)
                    for i in range(4):
                        e = act.activation(probs[:, k, i, :], pb[3 + i // 2][:, (i % 2) * P:(i % 2 + 1) * P],
                                           ACT.Exp, scale=ATTN_SCALE, bias=nmax[:, k, i:i + 1],
                                           accum_out=psum_[:, k, i:i + 1])
                        if i % 2:
                            e.then_inc(read[3 + i // 2], 1)
                    act.activation(esink[:, k, :], sarg[:, k, :], ACT.Exp).then_inc(probs_exp, 1)
                elif kind == "probs_t":
                    wait_full(act, g, last, step, 5)
                    if a >= 1:
                        wait_full(act, g, last, ("attend", a - 1, 0), 6)
                    act.activation(probs_t[:], pb[5][:].rearrange("p (i q) -> p i q", i=4),
                                   ACT.Copy).then_inc(read[5], 1)
                elif kind == "attend":
                    wait_full(act, g, last, step, 6)
                    act.activation(attn_o[:, a, :, :], pb[6][:, 0:A_GROUP * CHUNK].rearrange(
                        "p (j q) -> p j q", j=A_GROUP), ACT.Copy).then_inc(read[6], 1)
                elif kind in ("kend_t", "v_t"):
                    b = banks(step)[0]
                    dst = kend_tok if kind == "kend_t" else v_tok
                    wait_full(act, g, last, step, b)
                    if s == 0:
                        act.activation(dst[:, 0:4, :], pb[b][:].rearrange("p (i d) -> p i d", i=4),
                                       ACT.Copy).then_inc(read[b], 1)
                    else:
                        act.activation(dst[:, 4, :], pb[b][:, 0:P], ACT.Copy)
                        act.activation(dst[0:CHUNK, 5, :], pb[b][0:CHUNK, P:2 * P],
                                       ACT.Copy).then_inc(read[b], 1)
                elif kind == "read_out":
                    b = banks(step)[0]
                    lo, hi = (0, 512) if s == 0 else (512, T)
                    if s == 0:
                        act.wait_ge(first_made, B_HEADS * g + a + 1)
                        act.dma_start(state_first[g, a], s_first[:]).then_inc(first_out, 16)
                        act.wait_ge(last_made, START + B_HEADS * g + a + 1)
                        act.dma_start(state_last[g, a], carry_s[:, a, :]).then_inc(last_out, 16)
                    wait_full(act, g, last, step, b)
                    act.wait_ge(finished, START + B_HEADS * g + a)
                    act.activation(ob[:, lo:hi], pb[b][:, 0:hi - lo], ACT.Copy).then_inc(ob_copied, 1)
                    act.activation(sq[:, lo:hi], pb[b][:, 0:hi - lo], ACT.Square).then_inc(read[b], 1)
                    if s == 1:
                        for r in range(2):
                            wait_read(act, g, last, ("read_out", a, r), 7 - r)
                        act.activation(sq_hi[:], sq[:], ACT.Copy).then_inc(sq_high, 1)
                elif kind == "sum_sq":
                    b = banks(step)[0]
                    lo, hi = (0, 512) if s == 0 else (512, T)
                    wait_full(act, g, last, step, b)
                    act.activation(rs[:, lo:hi], pb[b][:, 0:hi - lo], ACT.Sqrt, scale=1.0 / P,
                                   bias=eps[:]).then_inc(read[b], 1)
                elif kind in ("ma", "mb"):
                    if s == 0:
                        ahead(f"{kind}{a}")
                    bank = bank_of(last, step)
                    lo, hi = sub(s)
                    dst = sig_a if kind == "ma" else sig_b
                    wait_full(act, g, last, step, bank)
                    if kind == "ma" and s == 0:
                        act.wait_ge(merged, START + 2 * MERGES * g + 2 * a)
                        if a == 0:
                            act.wait_ge(windows_out, 16 * 4 * (g + 1))
                    act.activation(dst[:, lo:hi], pb[bank][:, 0:hi - lo], ACT.Sigmoid).then_inc(read[bank], 1)
                elif kind == "ya" and s == 0:
                    ahead(f"wab{a}")
                elif kind == "out":
                    ahead(f"wo{a}{s}")
                    if (a, s) == (1, 3) and not last:
                        high(g + 1, 2)
                elif kind.startswith("x_"):
                    prepare_x(step, g, g + 1, last)
            if last:
                act.activation(root[:], eps[:], ACT.Sqrt)
            for i, (t0, n) in enumerate(TILES):
                act.wait_ge(summed, NT * g + i + 1)
                link(act.activation(scratch[0:n, :], res[0:n, i, :], ACT.Square,
                                    accum_out=yss[0:n, i:i + 1]))
                act.activation(yss[0:n, i:i + 1], yss[0:n, i:i + 1], ACT.Sqrt, scale=1.0 / D_MODEL,
                               bias=eps[0:n, :]).then_inc(y_root, 1)

        groups(act, body)

    @block.vector
    def _(dve):
        links = [0]

        def link(ins):
            links[0] += 1
            ins.then_inc(dve_step, 1)
            dve.wait_ge(dve_step, links[0])

        def prepare_x(step, g, gn, last):
            kind, s, _ = step
            lo, hi = sub(s)
            n = hi - lo
            if kind == "x_square":
                if s == 0:
                    add_squares(dve, 0, gn)
            elif kind == "x_split":
                rms = x_acc[:, s, 1, 0:n]
                wait_read(dve, g, last, ("x_sum", s, 0), 6 + s)
                link(dve.reciprocal(rms, rms))

                def x_low(q):
                    k = slice(2 * q, 2 * q + 2)
                    dve.wait_ge(x_high, 8 * gn + 4 * s + q + 1)
                    dve.tensor_tensor(x_lo[:, k, lo:hi], x_raw[:, k, lo:hi], x_hi[:, k, lo:hi].bitcast(F32),
                                      ALU.subtract).then_inc(x_split, 1)

                for q in range(4):
                    for kt in (2 * q, 2 * q + 1):
                        v = x_raw[:, kt, lo:hi]
                        ins = dve.scalar_tensor_tensor(out=v, in0=v, scalar=gain[:, kt:kt + 1], in1=rms,
                                                       op0=ALU.mult, op1=ALU.mult)
                    ins.then_inc(x_scaled, 1)
                    if q:
                        x_low(q - 1)
                x_low(3)

        dve.memset(eps[:], EPS)
        dve.memset(ones[:], 1.0)
        dve.memset(start_f[:], 0.0)
        link(dve.memset(end_one[:], 0.0))
        dve.tensor_copy(ones_r[:], ones[:])
        dve.memset(end_one[:, CHUNK - 1:T:CHUNK], 1.0).then_inc(consts_made, 1)
        dve.wait_ge(consts_made, 1)
        dve.wait_ge(logit_in, 16)
        link(dve.tensor_tensor(lb[:], logit[:, 0, :], logit[:, 1, :], ALU.max))
        dve.tensor_tensor(logit[:], logit[:], lb[:, None, :].broadcast_to([P, 2, 4]),
                          ALU.subtract).then_inc(lb_max, 1)
        dve.wait_ge(lb_exp, 1)
        link(dve.tensor_tensor(lb[:], logit[:, 0, :], logit[:, 1, :], ALU.add))
        link(dve.reciprocal(lb[:], lb[:]))
        link(dve.tensor_tensor(lb[:], lb[:], logit[:, 0, :], ALU.mult))
        link(dve.tensor_scalar(one_lb[:], lb[:], -1.0, 1.0, ALU.mult, ALU.add))
        dve.wait_ge(gain_in, 16)
        for step in X_STEPS:
            prepare_x(step, None, 0, False)
        dve.wait_ge(consts_in, 16 * 8)
        link(dve.tensor_scalar(neg_sink[:], sink[:], -1.0, None, ALU.mult))

        def split(hi, lo, val):
            link(dve.tensor_copy(hi, val))
            return dve.tensor_tensor(lo, val, hi.bitcast(F32), ALU.subtract)

        def final_norm(g, i):
            n = TILES[i][1]
            dve.wait_ge(y_root, NT * g + i + 1)
            link(dve.reciprocal(yss[0:n, i:i + 1], yss[0:n, i:i + 1]))
            dve.scalar_tensor_tensor(out=res[0:n, i, :], in0=res[0:n, i, :], scalar=yss[0:n, i:i + 1],
                                     in1=fgain[0:n, :], op0=ALU.mult, op1=ALU.mult).then_inc(y_made, 1)

        def rotate(dst, first):
            v = "p (c t) -> p c t"
            link(dve.tensor_tensor(dst, raw[:].rearrange(v, t=CHUNK), cos[:].rearrange(v, t=CHUNK), ALU.mult))
            link(dve.stream_shuffle(swap[:], raw[:], [i ^ (ROPE_DIM // 2) for i in range(32)]))
            dve.tensor_tensor(swap[:], swap[:], sin[:], ALU.mult).then_inc(raw_free, 1)
            dve.wait_ge(raw_free, START + first)
            return dve.tensor_tensor(dst, dst, swap[:].rearrange(v, t=CHUNK), ALU.add)

        def body(g, last):
            dve.sem_clear(dve_step)
            links[0] = 0
            for step in steps(last):
                kind, a, s = step
                if kind == "evac":
                    step = ("proj", a, s)
                    bank = bank_of(last, step)
                    lo, hi = sub(s)
                    src = pb[bank][:, 0:hi - lo]
                    n = a[:2]
                    if n == "ak" and s == 1:
                        wait_block_read(dve, g, last, a)
                        dve.wait_ge(rope_in, 32 * (g + 1))
                        link(dve.tensor_copy(k_rot[:, 0:CHUNK], carry_k[:]))
                        k = k_rot[:, CHUNK:].rearrange("p (c t) -> p c t", t=CHUNK)
                        link(rotate(k, 5 * g + 1))
                        dve.tensor_copy(carry_k[:], k_rot[:, T:T + CHUNK]).then_inc(k_roped, 1)
                        link(dve.tensor_copy(v_t[:, 0:CHUNK], carry_v[:]))
                        dve.sem_inc(carried, 1)
                    elif n == "av" and s == 1:
                        wait_read(dve, g, last, step, bank)
                        link(dve.tensor_copy(carry_v[:], v_t[:, T:T + CHUNK]))
                    elif n == "aq" and s == 1:
                        j = int(a[2:])
                        wait_block_read(dve, g, last, a)
                        if j == 0:
                            dve.wait_ge(y_out, START + 16 * NT * g)
                        rotate(q_rot[:, :, j, :], 5 * g + 2 + j).then_inc(q_roped, 1)
                        dve.wait_ge(q_roped, START + A_GROUP * g + j + 1)
                    elif n == "bf" and s == 1:
                        h = int(a[2:])
                        wait_block_read(dve, g, last, a)
                        link(dve.tensor_scalar(f[:, 0:T], f[:, 0:T], one_lb[:, h:h + 1], lb[:, h:h + 1],
                                               ALU.mult, ALU.add))
                        dve.tensor_scalar(keyb[:], f[:, 0:T], -1.0, 1.0, ALU.mult, ALU.add)
                        link(dve.tensor_copy(start_f[:, 0:T:CHUNK], f[:, 0:T:CHUNK]))
                        link(dve.memset(f[:, 0:T + 1:CHUNK], 0.0))
                        link(dve.tensor_tensor_scan(prod[:], f[:, 0:T], start_f[:], 0.0, ALU.mult, ALU.add))
                        link(dve.tensor_copy(decay[:, h, :], prod[:, CHUNK - 1:T:CHUNK]))
                    elif n == "bq":
                        h = int(a[2:])
                        wait_full(dve, g, last, step, bank)
                        dve.tensor_tensor(q_dec[:, h, lo:hi], src, prod[:, lo:hi], ALU.mult).then_inc(read[bank], 1)
                    elif n == "bg":
                        h = int(a[2:])
                        dve.wait_ge(sig_made, 16 * g + 2 * h + s + 1)
                        dve.tensor_tensor(gate_b[:, h, lo:hi], src, gate_b[:, h, lo:hi],
                                          ALU.mult).then_inc(read[bank], 1)
                    elif n == "ag":
                        j = int(a[2:])
                        c0, c1 = SUBS[s]
                        dve.wait_ge(sig_made, 16 * g + 2 * (B_HEADS + j) + s + 1)
                        v = raw[:, lo:hi]
                        dve.tensor_tensor(v, src, v, ALU.mult).then_inc(read[bank], 1)
                        wait_read(dve, g, last, step, bank)
                        vv = v.rearrange("p (c t) -> p c t", t=CHUNK)
                        if j == 0 and s == 0:
                            wait_read(dve, g, last, ("attend", NCH - 1, 0), 6)
                        link(dve.tensor_tensor(vv, vv, attn_o[:, c0:c1, j, :], ALU.mult))
                        split(ga_hi[:, c0:c1, j, :], ga_lo[:, c0:c1, j, :], vv).then_inc(gated_a, 1)
                elif kind == "keys":
                    h = a
                    if h:
                        wait_full(dve, g, last, ("kend_t", h - 1, 1), 6)
                        wait_full(dve, g, last, ("scores_b", h - 1, 1), 5)
                    dve.tensor_tensor_scan(rev[:, ::-1], f[:, T:0:-1], end_one[:, ::-1],
                                           0.0, ALU.mult, ALU.add).then_inc(f_used, 1)
                    link(dve.reciprocal(inv[:], prod[:]))
                    dve.wait_ge(f_used, START + B_HEADS * g + h + 1)
                    link(dve.tensor_tensor(inv[:], inv[:], keyb[:], ALU.mult))
                    link(dve.tensor_tensor(rev[:], rev[:], keyb[:], ALU.mult))
                    dve.sem_inc(keys_made, 1)
                elif kind == "scores":
                    c, k = a, a % 2
                    wait_full(dve, g, last, step, 3)
                    wait_full(dve, g, last, step, 4)
                    if c >= 2:
                        dve.wait_ge(probs_exp, NCH * g + c - 1)
                    if c == 1:
                        dve.wait_ge(flags_in, 32 * (g + 1))
                        for b in (3, 4):
                            v = pb[b][:, 0:2 * P].rearrange("p (i k) -> p i k", i=2)[:, :, 0:CHUNK]
                            link(dve.tensor_scalar(v, v, amask[:, 0:1], None, ALU.add))
                    for b in (3, 4):
                        link(dve.tensor_reduce(rmax[:, k, 2 * (b - 3):2 * (b - 3) + 2],
                                               pb[b][:, 0:2 * P].rearrange("p (i k) -> p i k", i=2),
                                               AX.X, ALU.max))
                    link(dve.scalar_tensor_tensor(out=nmax[:, k, :], in0=rmax[:, k, :], scalar=-ATTN_SCALE,
                                                  in1=neg_sink[:], op0=ALU.mult, op1=ALU.min))
                    dve.tensor_tensor(sarg[:, k, :], sink[:], nmax[:, k, :], ALU.add).then_inc(row_max, 1)
                elif kind == "normalise":
                    c, k = a, a % 2
                    dve.wait_ge(probs_exp, NCH * g + c + 1)
                    link(dve.tensor_tensor(rden[:, k, :], psum_[:, k, :], esink[:, k, :], ALU.add))
                    link(dve.reciprocal(rden[:, k, :], rden[:, k, :]))
                    dve.tensor_tensor(probs[:, k, :, :], probs[:, k, :, :],
                                      rden[:, k, :, None].broadcast_to([P, 4, P]),
                                      ALU.mult).then_inc(probs_norm, 1)
                elif kind == "scores_b":
                    h, b = a, banks(step)[0]
                    if h == 0 and s == 0:
                        wait_full(dve, g, last, step, b)
                        link(dve.memset(sc_t[:], 0.0))
                    if h and s == 0:
                        wait_full(dve, g, last, ("read_out", h - 1, 1), 6)
                    wait_full(dve, g, last, step, b)
                    link(dve.memset(pad[:], 0.0))
                    if s == 0:
                        dve.copy_predicated(sc_t[:, 0:4, :], caus[:, None, :].broadcast_to([P, 4, P]),
                                            pb[b][:].rearrange("p (i t) -> p i t", i=4)).then_inc(read[b], 1)
                    else:
                        dve.copy_predicated(sc_t[:, 4, :], caus[:], pb[b][:, 0:P])
                        dve.copy_predicated(sc_t[0:CHUNK, 5, 0:CHUNK], caus[0:CHUNK, 0:CHUNK],
                                            pb[b][0:CHUNK, P:P + CHUNK]).then_inc(read[b], 1)
                elif kind == "update":
                    h = a
                    if h:
                        wait_full(dve, g, last, ("read_out", h - 1, 1), 6)
                    dve.wait_ge(first_out, START + 16 * (B_HEADS * g + h))
                    dve.wait_ge(last_out, START + 16 * (B_HEADS * g + h))
                    link(dve.tensor_copy(st[:, 0, :], carry_s[:, h, :]))
                    for c in range(NCH):
                        b = UPDATE_BANK[c]
                        i = UPDATE_BANKS[b].index(c)
                        if i == 0:
                            wait_full(dve, g, last, step, b)
                        dst = carry_s[:, h, :] if c == NCH - 1 else s_first[:] if c == 0 else st[:, c + 1, :]
                        ins = dve.scalar_tensor_tensor(
                            out=dst, in0=st[:, c, :], scalar=decay[:, h, c:c + 1],
                            in1=pb[b][:, i * P:(i + 1) * P], op0=ALU.mult, op1=ALU.add)
                        if c == 0:
                            ins.then_inc(first_made, 1)
                            dve.wait_ge(first_made, B_HEADS * g + h + 1)
                            dve.wait_ge(flags_in, 32 * (g + 1))
                            link(dve.memset(st[:, 1, :], 0.0))
                            link(dve.copy_predicated(st[:, 1, :], keep[:].broadcast_to([P, P]), s_first[:]))
                        elif c == NCH - 1:
                            ins.then_inc(last_made, 1)
                            dve.wait_ge(last_made, START + B_HEADS * g + h + 1)
                            dve.sem_inc(read[b], 1)
                        elif c == UPDATE_BANKS[b][-1]:
                            ins.then_inc(read[b], 1)
                            wait_read(dve, g, last, step, b)
                        else:
                            link(ins)
                elif kind == "read_out" and s == 1:
                    dve.wait_ge(sq_high, B_HEADS * g + a + 1)
                    dve.tensor_tensor(sq_lo[:], sq[:], sq_hi[:].bitcast(F32), ALU.subtract).then_inc(sq_split, 1)
                elif kind == "finish":
                    h = a
                    wait_read(dve, g, last, ("sum_sq", h, 0), 7)
                    wait_read(dve, g, last, ("sum_sq", h, 1), 5)
                    dve.wait_ge(ob_copied, 2 * (B_HEADS * g + h + 1))
                    wait_block_read(dve, g, last, f"bg{h}")
                    link(dve.reciprocal(rs[:], rs[:]))
                    link(dve.scalar_tensor_tensor(out=ob[:], in0=ob[:], scalar=gain_b[:, h:h + 1], in1=rs[:],
                                                  op0=ALU.mult, op1=ALU.mult))
                    link(dve.tensor_tensor(ob[:], ob[:], gate_b[:, h, :], ALU.mult))
                    split(gb_hi[:, h, :], gb_lo[:, h, :], ob[:]).then_inc(finished, 1)
                elif kind == "ya":
                    bank = bank_of(last, step)
                    lo, hi = sub(s)
                    wait_full(dve, g, last, step, bank)
                    wait_read(dve, g, last, ("ma", a, s), bank_of(last, ("ma", a, s)))
                    dve.tensor_tensor(sig_a[:, lo:hi], sig_a[:, lo:hi], pb[bank][:, 0:hi - lo],
                                      ALU.mult).then_inc(read[bank], 1)
                elif kind == "yb":
                    bank = bank_of(last, step)
                    lo, hi = sub(s)
                    wait_full(dve, g, last, step, bank)
                    wait_read(dve, g, last, ("mb", a, s), bank_of(last, ("mb", a, s)))
                    dve.tensor_tensor(sig_b[:, lo:hi], sig_b[:, lo:hi], pb[bank][:, 0:hi - lo],
                                      ALU.mult).then_inc(read[bank], 1)
                    wait_read(dve, g, last, step, bank)
                    wait_read(dve, g, last, ("ya", a, s), bank_of(last, ("ya", a, s)))
                    link(dve.tensor_tensor(sig_a[:, lo:hi], sig_a[:, lo:hi], sig_b[:, lo:hi], ALU.add))
                    if a == 0 and s == 0:
                        dve.wait_ge(finished, START + B_HEADS * (g + 1))
                    split(m_hi[:, a, lo:hi], m_lo[:, a, lo:hi], sig_a[:, lo:hi]).then_inc(merged, 1)
                elif kind == "out" and s == 3:
                    for i, (t0, n) in enumerate(TILES):
                        b = OUT_BANKS[i]
                        r = res[0:n, i, 512 * a:512 * a + 512]
                        wait_full(dve, g, last, ("out", a, 0), b)
                        dve.wait_ge(res_in[i], 16 * (g + 1))
                        dve.tensor_tensor(r, r, pb[b][0:n, :], ALU.add).then_inc(read[b], 1)
                        if a == 1:
                            wait_read(dve, g, last, ("out", 1, 0), b)
                            dve.sem_inc(summed, 1)
                            if i > 1 and last:
                                final_norm(g, i - 2)
                elif kind.startswith("x_"):
                    prepare_x(step, g, g + 1, last)
            for i in range(NT - 2 if last else 0, NT):
                final_norm(g, i)

        groups(dve, body)

    @block.tensor
    def _(pe):
        def three_pass(out, w_h, w_l, m_h, m_l, first, last_of_bank):
            pe.matmul(out, w_h, m_h, start=first, stop=False)
            pe.matmul(out, w_h, m_l, start=False, stop=False)
            return pe.matmul(out, w_l, m_h, start=False, stop=last_of_bank)

        def prepare_x(step, g, gn, last):
            kind, s, _ = step
            if kind == "x_sum":
                lo, hi = sub(s)
                b = 6 + s
                pe.wait_ge(x_summed[s], gn + 1)
                wait_bank_free(pe, g, last, step, b)
                pe.matmul(pb[b][:, 0:hi - lo], ones[:], x_acc[:, s, 0, 0:hi - lo],
                          start=True, stop=True).then_inc(full[b], 1)

        pe.wait_ge(consts_made, 1)
        for step in X_STEPS:
            prepare_x(step, None, 0, False)

        def body(g, last):
            for step in steps(last):
                kind, a, s = step
                if kind == "proj" or kind in ("ma", "mb"):
                    b = BLOCK[a if kind == "proj" else f"{kind}{a}"]
                    bank = bank_of(last, step)
                    lo, hi = sub(s)
                    if s == 0:
                        pe.wait_ge(w_split, NB * g + b + 1)
                    wait_bank_free(pe, g, last, step, bank)
                    for k in range(KT):
                        if a == "ak" and k % 2 == 0:
                            pe.wait_ge(x_split, 8 * g + 4 * s + k // 2 + 1)
                        ins = three_pass(pb[bank][:, 0:hi - lo], w_hi[SLOT[b]][:, k, :], w_lo[SLOT[b]][:, k, :],
                                         x_hi[:, k, lo:hi], x_lo[:, k, lo:hi], k == 0, k == KT - 1)
                    ins.then_inc(full[bank], 1)
                elif kind in ("ya", "yb"):
                    b = BLOCK[f"wab{a}"]
                    bank = bank_of(last, step)
                    lo, hi = sub(s)
                    c0, c1 = SUBS[s]
                    if s == 0:
                        pe.wait_ge(w_split, NB * g + b + 1)
                        if kind == "ya":
                            pe.wait_ge(gated_a, START + 2 * A_GROUP * (g + 1))
                        else:
                            pe.wait_ge(finished, START + B_HEADS * (g + 1))
                    wait_bank_free(pe, g, last, step, bank)
                    for k in range(4):
                        if kind == "ya":
                            out = pb[bank][:, 0:hi - lo].rearrange("p (c t) -> p c t", t=CHUNK)
                            m_h, m_l = ga_hi[:, c0:c1, k, :], ga_lo[:, c0:c1, k, :]
                        else:
                            out = pb[bank][:, 0:hi - lo]
                            m_h, m_l = gb_hi[:, k, lo:hi], gb_lo[:, k, lo:hi]
                        kk = k + 4 * (kind == "yb")
                        ins = three_pass(out, w_hi[SLOT[b]][:, kk, :], w_lo[SLOT[b]][:, kk, :],
                                         m_h, m_l, k == 0, k == 3)
                    ins.then_inc(full[bank], 1)
                elif kind == "v_win":
                    cs = range(4 * a, min(4 * a + 4, NCH))
                    if a == 0:
                        pe.wait_ge(consts_in, 16 * 8)
                        pe.wait_ge(carried, g + 1)
                        wait_block_read(pe, g, last, "av")
                    bank = banks(step)[0]
                    wait_bank_free(pe, g, last, step, bank)
                    for i, c in enumerate(cs):
                        ins = pe.transpose(pb[bank][:, i * P:(i + 1) * P], v_t[:, c * CHUNK:c * CHUNK + P], ident[:])
                    ins.then_inc(full[bank], 1)
                elif kind == "k_win":
                    pe.wait_ge(k_roped, g + 1)
                    wait_bank_free(pe, g, last, step, 4)
                    for i, c in enumerate((0, NCH - 1)):
                        ins = pe.transpose(pb[4][:, i * P:(i + 1) * P], k_rot[:, c * CHUNK:c * CHUNK + P], ident[:])
                    ins.then_inc(full[4], 1)
                elif kind == "scores":
                    c = a
                    if c == 0:
                        pe.wait_ge(q_roped, START + A_GROUP * (g + 1))
                    for v in range(A_KV):
                        wait_bank_free(pe, g, last, step, 3 + v)
                    for i in range(2):
                        for v in range(A_KV):
                            rows = slice(HEAD_DIM * v, HEAD_DIM * (v + 1))
                            ins = pe.matmul(pb[3 + v][:, i * P:(i + 1) * P],
                                            q_rot[rows, c, 2 * i:2 * i + 2, :],
                                            k_rot[rows, c * CHUNK:c * CHUNK + P], start=True, stop=True)
                            if i == 1:
                                ins.then_inc(full[3 + v], 1)
                elif kind == "probs_t":
                    pe.wait_ge(probs_norm, NCH * g + a + 1)
                    wait_bank_free(pe, g, last, step, 5)
                    for i in range(4):
                        ins = pe.transpose(pb[5][:, i * P:(i + 1) * P], probs[:, a % 2, i, :], ident[:])
                    ins.then_inc(full[5], 1)
                elif kind == "attend":
                    wait_read(pe, g, last, ("probs_t", a, 0), 5)
                    if a == 0:
                        wait_read(pe, g, last, ("v_win", 2, 0), 5)
                    wait_bank_free(pe, g, last, step, 6)
                    for v in range(A_KV):
                        rows = slice(HEAD_DIM * v, HEAD_DIM * (v + 1))
                        ins = pe.matmul(pb[6][rows, 0:2 * P], v_win[:, a, rows], probs_t[:, 2 * v:2 * v + 2, :],
                                        start=True, stop=True)
                    ins.then_inc(full[6], 1)
                elif kind in ("kend_t", "v_t"):
                    b = banks(step)[0]
                    src = rev if kind == "kend_t" else vb
                    if s == 0:
                        if kind == "kend_t":
                            pe.wait_ge(keys_made, B_HEADS * g + a + 1)
                        else:
                            wait_block_read(pe, g, last, f"bi{a}")
                    wait_bank_free(pe, g, last, step, b)
                    for k, i in enumerate(range(4) if s == 0 else (4, 5)):
                        t0, n = TILES[i]
                        ins = pe.transpose(pb[b][0:n, k * P:(k + 1) * P], src[:, t0:t0 + n], ident[:])
                    ins.then_inc(full[b], 1)
                elif kind == "scores_b":
                    b = banks(step)[0]
                    if s == 0:
                        wait_block_read(pe, g, last, f"bq{a}")
                    wait_bank_free(pe, g, last, step, b)
                    for k, i in enumerate(range(4) if s == 0 else (4, 5)):
                        t0, n = TILES[i]
                        ins = pe.matmul(pb[b][0:n, k * P:k * P + n], inv[:, t0:t0 + n], q_dec[:, a, t0:t0 + n],
                                        start=True, stop=True)
                    ins.then_inc(full[b], 1)
                elif kind == "update":
                    wait_read(pe, g, last, ("v_t", a, 0), 7)
                    wait_read(pe, g, last, ("v_t", a, 1), 6)
                    for c in range(NCH):
                        b = UPDATE_BANK[c]
                        i = UPDATE_BANKS[b].index(c)
                        if i == 0:
                            wait_bank_free(pe, g, last, step, b)
                        rows = slice(CHUNK * (c % 2), CHUNK * (c % 2 + 1))
                        ins = pe.matmul(pb[b][:, i * P:(i + 1) * P], kend_tok[rows, c // 2, :],
                                        v_tok[rows, c // 2, :], start=True, stop=True)
                        if c == UPDATE_BANKS[b][-1]:
                            ins.then_inc(full[b], 1)
                elif kind == "read_out":
                    b = banks(step)[0]
                    if s == 0:
                        pe.wait_ge(last_made, START + B_HEADS * g + a + 1)
                        wait_read(pe, g, last, ("scores_b", a, 1), 5)
                    wait_bank_free(pe, g, last, step, b)
                    tiles = range(4) if s == 0 else (4, 5)
                    for k, i in enumerate(tiles):
                        n = TILES[i][1]
                        pe.matmul(pb[b][:, k * P:k * P + n], v_tok[0:n, i, :], sc_t[0:n, i, 0:n],
                                  start=(k == 0), stop=False, skip_group_check=True)
                    chunks = range(8) if s == 0 else range(8, NCH)
                    for k, c in enumerate(chunks):
                        ins = pe.matmul(pb[b][:, k * CHUNK:(k + 1) * CHUNK], st[:, c, :],
                                        q_dec[:, a, c * CHUNK:(c + 1) * CHUNK],
                                        start=False, stop=(c == chunks[-1]), skip_group_check=True)
                    ins.then_inc(full[b], 1)
                elif kind == "sum_sq":
                    b = banks(step)[0]
                    lo, hi = (0, 512) if s == 0 else (512, T)
                    pe.wait_ge(sq_split, B_HEADS * g + a + 1)
                    wait_bank_free(pe, g, last, step, b)
                    pe.matmul(pb[b][:, 0:hi - lo], ones_r[:], sq_hi[:, lo:hi], start=True, stop=False)
                    pe.matmul(pb[b][:, 0:hi - lo], ones_r[:], sq_lo[:, lo:hi],
                              start=False, stop=True).then_inc(full[b], 1)
                elif kind == "out":
                    b = BLOCK[f"wo{a}{s}"]
                    pe.wait_ge(w_split, NB * g + b + 1)
                    if a == 0:
                        pe.wait_ge(merged, START + 2 * MERGES * g + 4 * (s + 1))
                    wh = w_hi[SLOT[b]][:].rearrange("p k c -> p (k c)")
                    wl = w_lo[SLOT[b]][:].rearrange("p k c -> p (k c)")
                    for i, (t0, n) in enumerate(TILES):
                        bank = OUT_BANKS[i]
                        if s == 0:
                            wait_bank_free(pe, g, last, step, bank)
                        for k in range(2):
                            kt = 2 * s + k
                            mh, ml = m_hi[:, kt, t0:t0 + n], m_lo[:, kt, t0:t0 + n]
                            cols = slice(512 * k, 512 * k + 512)
                            pe.matmul(pb[bank][0:n, :], mh, wh[:, cols], start=(kt == 0), stop=False)
                            pe.matmul(pb[bank][0:n, :], mh, wl[:, cols], start=False, stop=False)
                            ins = pe.matmul(pb[bank][0:n, :], ml, wh[:, cols], start=False, stop=(kt == KT - 1))
                        if s == 3:
                            ins.then_inc(full[bank], 1)
                    pe.drain().then_inc(piece_used, 1)
                elif kind.startswith("x_"):
                    prepare_x(step, g, g + 1, last)

        groups(pe, body)

    ctx.close()


def rope_tables():
    import numpy as np
    half = ROPE_DIM // 2
    inv = np.power(np.float32(ROPE_THETA), -np.arange(half, dtype=np.float32) * np.float32(2.0 / ROPE_DIM))
    pos = np.concatenate([PAST_LEN + np.arange(DEC_SEQ), np.arange(SEQ)]).astype(np.float32)
    ang = (inv.astype(np.float32)[:, None] * pos[None, :]).astype(np.float32).astype(np.float64)
    cos = np.ones((HEAD_DIM, pos.size), np.float32)
    sin = np.zeros((HEAD_DIM, pos.size), np.float32)
    cos[:half], cos[half:ROPE_DIM] = np.cos(ang), np.cos(ang)
    sin[:half], sin[half:ROPE_DIM] = -np.sin(ang), np.sin(ang)
    return [np.ascontiguousarray(np.tile(t, (A_KV, 1)).reshape(P, GROUPS, T).transpose(1, 0, 2))
            for t in (cos, sin)]


def layouts(i):
    import numpy as np
    w_in, w_ba, w_bb, w_out = i["w_in"][0], i["w_branch_a"][0], i["w_branch_b"][0], i["w_out"][0]

    def heads(rows):
        return rows.reshape(A_KV, A_GROUP, HEAD_DIM, -1).transpose(1, 0, 2, 3).reshape(A_GROUP, P, -1)

    def tiled(cols):
        return cols.reshape(KT, P, P).transpose(1, 0, 2)

    cut = np.split(w_in, np.cumsum([512, 128, 128, 512, 512, 512, 512, 512, D_MODEL]), axis=1)
    names = ["aq", "ak", "av", "ag", "bq", "bf", "bi", "bg", "ma", "mb"]
    cut = dict(zip(names, cut))
    by_head = {n: heads(np.ascontiguousarray(cut[n].T)) for n in ("aq", "ag")}
    w_a = heads(w_ba)
    w_b = w_bb.reshape(B_HEADS, P, D_MODEL)
    blocks = []
    for n in BLOCKS:
        if n in ("ak", "av"):
            blocks.append(tiled(cut[n]))
        elif n[:2] in ("aq", "ag"):
            blocks.append(tiled(by_head[n[:2]][int(n[2:])].T))
        elif n.startswith("wab"):
            c = slice(P * int(n[3:]), P * (int(n[3:]) + 1))
            blocks.append(np.concatenate([w_a[:, :, c], w_b[:, :, c]]).transpose(1, 0, 2))
        elif n.startswith("wo"):
            hf, kp = int(n[2]), int(n[3])
            rows = w_out[2 * P * kp:2 * P * (kp + 1), 512 * hf:512 * (hf + 1)]
            blocks.append(rows.reshape(2, P, 512).transpose(1, 0, 2).reshape(P, KT, P))
        else:
            c = slice(P * int(n[2:]), P * (int(n[2:]) + 1))
            blocks.append(tiled(cut[n[:2]][:, c]))
    x = np.concatenate([i["x_sample"][0], i["x_prompt"][0]]).reshape(GROUPS, T, D_MODEL)
    old = WINDOW - CHUNK
    cache_k = i["cache_attn_k"][0, 0, old:].reshape(CHUNK, P).T
    cache_v = i["cache_attn_v"][0, 0, old:].reshape(CHUNK, P).T
    j = np.arange(P)[:, None] // CHUNK
    col = np.arange(4)[None, :]
    sinks = i["attn_sinks"][0][(col // 2) * A_GROUP + 2 * (col % 2) + j]
    cos, sin = rope_tables()
    tok = np.arange(P)
    causal = ((tok[:, None] <= tok[None, :]) & (tok[:, None] // CHUNK == tok[None, :] // CHUNK))
    first = np.zeros((GROUPS, P, 1), np.float32)
    first[0] = NEG_INF
    keep = np.ones((GROUPS, P, 1), np.int32)
    keep[0] = 0
    return {
        "x": x, "x_t": x.reshape(GROUPS, T, KT, P).transpose(0, 3, 2, 1), "w": np.stack(blocks),
        "cache_k": cache_k, "cache_v": cache_v,
        "state": i["state_hgrn"][0, 0].transpose(1, 0, 2),
        "norm_gain": i["norm_gain"][0].reshape(KT, P).T, "sinks": sinks,
        "lb_logits": i["hgrn_lb_logits"].reshape(2, B_HEADS, P).transpose(2, 0, 1),
        "hgrn_gain": i["hgrn_norm_gain"][0].reshape(B_HEADS, P).T,
        "final_gain": np.broadcast_to(i["final_norm_gain"], (P, D_MODEL)),
        "rope_cos": cos, "rope_sin": sin, "causal": causal.astype(np.int32),
        "identity": np.eye(P, dtype=np.float32), "first_mask": first, "keep_state": keep,
    }


OUTPUTS = {
    "y": (GROUPS, T, D_MODEL), "win_k": (GROUPS, 2, P, P), "win_v": (GROUPS, 2, P, P),
    "state_first": (GROUPS, B_HEADS, P, P), "state_last": (GROUPS, B_HEADS, P, P),
}


def kernel(**inputs):
    import numpy as np
    from concourse import bacc
    from concourse.bass_utils import run_bass_kernel_spmd

    arrays = {n: np.ascontiguousarray(a) for n, a in layouts({k: np.asarray(v) for k, v in inputs.items()}).items()}
    nc = bacc.Bacc("TRN2", target_bir_lowering=False, num_devices=1)
    args = {n: nc.dram_tensor(f"in_{n}", a.shape, mybir.dt.from_np(a.dtype), kind="ExternalInput").ap()
            for n, a in arrays.items()}
    outs = {n: nc.dram_tensor(f"out_{n}", shape, F32, kind="ExternalOutput").ap() for n, shape in OUTPUTS.items()}
    program(nc, **args, **outs)
    r = run_bass_kernel_spmd(nc, [{f"in_{n}": a for n, a in arrays.items()}], core_ids=[0]).results[0]
    got = {n: r[f"out_{n}"] for n in OUTPUTS}
    y = got["y"].reshape(DEC_SEQ + SEQ, D_MODEL)
    window = (1, 1, WINDOW, A_KV, HEAD_DIM)
    return (y[DEC_SEQ:].reshape(1, SEQ, D_MODEL), y[:DEC_SEQ].reshape(1, DEC_SEQ, D_MODEL),
            got["win_k"][-1, 1].reshape(window), got["win_v"][-1, 1].reshape(window),
            got["state_last"][-1][None, None],
            got["win_k"][0, 0].reshape(window), got["win_v"][0, 0].reshape(window),
            got["state_first"][0][None, None])
```
